# Optimizing a Trainium2 kernel written in Bass

```python
import jax, jax.numpy as jnp
from jax import lax
import numpy as np

D_MODEL = 1024
BATCH = 1
SEQ = 256
DEPTH = 2
DEC_BATCH = 8
DEC_SEQ = 4
PAST_LEN = 1024
PAGE_SIZE = 128

N_MIXERS = 2
N_ATTN_LAYERS = (DEPTH + 1) // 2
N_SGU_LAYERS = DEPTH // 2
N_HEADS = 8
QK_NOPE = 128
QK_ROPE = 64
V_HEAD = 128
Q_LORA = 384
KV_LORA = 256
ROPE_THETA = 10000.0
SOFTMAX_SCALE = (QK_NOPE + QK_ROPE) ** -0.5
QUERY_BLOCK = 128
SGU_CHUNK = 128
SGU_HALF = 3 * D_MODEL
SGU_GROUPS = 8
SGU_GROUP_DIM = SGU_HALF // SGU_GROUPS
N_EXPERT_GROUPS = 4
EXPERTS_PER_GROUP = 8
N_EXPERTS = N_EXPERT_GROUPS * EXPERTS_PER_GROUP
TOP_K_EXPERTS = 2
EXPERT_HIDDEN = 256
PLE_DIM = 256
RMS_EPS = 1e-6
LN_EPS = 1e-5
NEG_INF = -1e30

kernel_name = 'hybrid_mla_chunkgmlp_hmoe_step'

def _rmsnorm(x, g):
    xf = x.astype(jnp.float32)
    y = xf * lax.rsqrt(jnp.mean(xf * xf, axis=-1, keepdims=True) + RMS_EPS)
    return (y * g.astype(jnp.float32)).astype(x.dtype)

def _layernorm(x, g, b):
    xf = x.astype(jnp.float32)
    mu = jnp.mean(xf, axis=-1, keepdims=True)
    var = jnp.mean(jnp.square(xf - mu), axis=-1, keepdims=True)
    y = (xf - mu) * lax.rsqrt(var + LN_EPS)
    return (y * g.astype(jnp.float32) + b.astype(jnp.float32)).astype(x.dtype)

def _rope(x, pos):
    half = QK_ROPE // 2
    inv_freq = 1.0 / (ROPE_THETA ** (jnp.arange(0, QK_ROPE, 2, dtype=jnp.float32) / QK_ROPE))
    ang = pos.astype(jnp.float32)[:, None] * inv_freq[None, :]
    bshape = (pos.shape[0],) + (1,) * (x.ndim - 3) + (half,)
    cos = jnp.cos(ang).reshape(bshape)
    sin = jnp.sin(ang).reshape(bshape)
    xf = x.astype(jnp.float32)
    x1, x2 = xf[..., :half], xf[..., half:]
    return jnp.concatenate([x1 * cos - x2 * sin, x2 * cos + x1 * sin], axis=-1).astype(x.dtype)

def _mla_project(hn, pos, w_in, g_q, g_kv, w_qb, w_uk):
    a = hn @ w_in
    cq = _rmsnorm(a[..., :Q_LORA], g_q)
    ckv = _rmsnorm(a[..., Q_LORA:Q_LORA + KV_LORA], g_kv)
    krope = _rope(a[..., Q_LORA + KV_LORA:], pos)
    q = (cq @ w_qb).reshape(cq.shape[:-1] + (N_HEADS, QK_NOPE + QK_ROPE))
    q_lat = jnp.einsum('bshn,chn->bshc', q[..., :QK_NOPE], w_uk)
    q_rope = _rope(q[..., QK_NOPE:], pos)
    return q_lat, q_rope, ckv, krope

def _mla_output(o_lat, w_uv, w_o):
    o = jnp.einsum('bshc,chv->bshv', o_lat, w_uv)
    return o.reshape(o.shape[:2] + (N_HEADS * V_HEAD,)) @ w_o

def _mla_prompt_attend(q_lat, q_rope, ckv, krope):
    b, s, h, c = q_lat.shape
    nb = s // QUERY_BLOCK
    ql = q_lat.reshape(b, nb, QUERY_BLOCK, h, c).transpose(1, 0, 2, 3, 4)
    qr = q_rope.reshape(b, nb, QUERY_BLOCK, h, QK_ROPE).transpose(1, 0, 2, 3, 4)
    qpos = jnp.arange(s, dtype=jnp.int32).reshape(nb, QUERY_BLOCK)
    kpos = jnp.arange(s, dtype=jnp.int32)

    def one_block(args):
        qlb, qrb, qp = args
        sc = (jnp.einsum('bqhc,bkc->bhqk', qlb, ckv)
              + jnp.einsum('bqhr,bkr->bhqk', qrb, krope)).astype(jnp.float32) * SOFTMAX_SCALE
        sc = jnp.where(kpos[None, None, None, :] <= qp[None, None, :, None], sc, NEG_INF)
        pr = jax.nn.softmax(sc, axis=-1).astype(ckv.dtype)
        return jnp.einsum('bhqk,bkc->bqhc', pr, ckv)

    out = lax.map(one_block, (ql, qr, qpos))
    return out.transpose(1, 0, 2, 3, 4).reshape(b, s, h, c)

def _mla_sample_attend(q_lat, q_rope, ckv_new, krope_new, ckv_past, krope_past):
    n_new = q_lat.shape[1]
    n_past = ckv_past.shape[1]
    s_past = (jnp.einsum('bqhc,bkc->bhqk', q_lat, ckv_past)
              + jnp.einsum('bqhr,bkr->bhqk', q_rope, krope_past)).astype(jnp.float32) * SOFTMAX_SCALE
    s_new = (jnp.einsum('bqhc,bkc->bhqk', q_lat, ckv_new)
             + jnp.einsum('bqhr,bkr->bhqk', q_rope, krope_new)).astype(jnp.float32) * SOFTMAX_SCALE
    causal = jnp.tril(jnp.ones((n_new, n_new), dtype=bool))
    s_new = jnp.where(causal[None, None], s_new, NEG_INF)
    pr = jax.nn.softmax(jnp.concatenate([s_past, s_new], axis=-1), axis=-1).astype(ckv_new.dtype)
    return (jnp.einsum('bhqk,bkc->bqhc', pr[..., :n_past], ckv_past)
            + jnp.einsum('bhqk,bkc->bqhc', pr[..., n_past:], ckv_new))

def _sgu_project(hn, w_in, b_in, g_v, b_v):
    z = jax.nn.gelu(hn @ w_in + b_in)
    u, v = jnp.split(z, 2, axis=-1)
    return u, _layernorm(v, g_v, b_v)

def _spatial_gate(v, w_s, b_s):
    b, n, l, _ = v.shape
    vg = v.reshape(b, n, l, SGU_GROUPS, SGU_GROUP_DIM)
    tril = jnp.tril(jnp.ones((SGU_CHUNK, SGU_CHUNK), dtype=bool))
    wm = jnp.where(tril[None], w_s, 0.0).astype(v.dtype)[:, :l, :l]
    s = jnp.einsum('grt,bntgc->bnrgc', wm, vg) + b_s[:, :l].T[:, :, None]
    return s.reshape(b, n, l, SGU_HALF)

def _hier_moe(hn, w_rg, b_rg, w_re, b_re, w_gate, w_up, w_down):
    lead = hn.shape[:-1]
    t = hn.reshape(-1, D_MODEL)
    n_tok = t.shape[0]
    pg = jax.nn.softmax((t @ w_rg + b_rg).astype(jnp.float32), axis=-1)
    pg_top, g_idx = lax.top_k(pg, 1)
    le = (t @ w_re + b_re).astype(jnp.float32).reshape(n_tok, N_EXPERT_GROUPS, EXPERTS_PER_GROUP)
    le_g = jnp.take_along_axis(le, g_idx[:, :, None], axis=1)[:, 0]
    pe = jax.nn.softmax(le_g, axis=-1)
    pe_top, e_idx = lax.top_k(pe, TOP_K_EXPERTS)
    w = pg_top * pe_top / jnp.sum(pe_top, axis=-1, keepdims=True)
    eid = g_idx * EXPERTS_PER_GROUP + e_idx
    gates = jnp.sum(jax.nn.one_hot(eid, N_EXPERTS, dtype=jnp.float32) * w[..., None], axis=1)
    h1 = jnp.einsum('td,edf->tef', t, w_gate)
    h2 = jnp.einsum('td,edf->tef', t, w_up)
    a = jax.nn.silu(h1) * h2 * gates[:, :, None].astype(t.dtype)
    y = jnp.einsum('tef,efd->td', a, w_down)
    return y.reshape(lead + (D_MODEL,))

def _ple(h, p_i, g, w_proj, w_gate):
    return jax.nn.sigmoid(_rmsnorm(h, g) @ w_gate) * (p_i @ w_proj)

def setup_inputs(seed: int = 0) -> dict:
    key = jax.random.key(seed)
    ks = iter(jax.random.split(key, 48))
    nrm = lambda shape, scale: jax.random.normal(next(ks), shape, jnp.float32) * scale
    gain = lambda shape: 1.0 + 0.02 * jax.random.normal(next(ks), shape, jnp.float32)
    n_pages = PAST_LEN // PAGE_SIZE
    n_used = DEC_BATCH * n_pages
    n_phys = n_used + max(1, n_used // 4)
    d = D_MODEL
    inp = {}
    inp['x_prompt'] = nrm((BATCH, SEQ, d), 1.0)
    inp['x_sample'] = nrm((DEC_BATCH, DEC_SEQ, d), 1.0)
    inp['cache_ckv'] = nrm((N_ATTN_LAYERS, n_phys, PAGE_SIZE, KV_LORA), 1.0)
    inp['cache_krope'] = nrm((N_ATTN_LAYERS, n_phys, PAGE_SIZE, QK_ROPE), 1.0)
    inp['page_table'] = jax.random.permutation(next(ks), n_phys)[:n_used].reshape(DEC_BATCH, n_pages).astype(jnp.int32)
    inp['p_prompt'] = nrm((DEPTH, BATCH, SEQ, PLE_DIM), 1.0)
    inp['p_sample'] = nrm((DEPTH, DEC_BATCH, DEC_SEQ, PLE_DIM), 1.0)
    inp['g_mix'] = gain((DEPTH, d))
    inp['g_ffn'] = gain((DEPTH, d))
    inp['g_ple'] = gain((DEPTH, d))
    inp['g_final'] = gain((d,))
    inp['mla_w_in'] = nrm((N_ATTN_LAYERS, d, Q_LORA + KV_LORA + QK_ROPE), d ** -0.5)
    inp['mla_g_q'] = gain((N_ATTN_LAYERS, Q_LORA))
    inp['mla_g_kv'] = gain((N_ATTN_LAYERS, KV_LORA))
    inp['mla_w_qb'] = nrm((N_ATTN_LAYERS, Q_LORA, N_HEADS * (QK_NOPE + QK_ROPE)), Q_LORA ** -0.5)
    inp['mla_w_uk'] = nrm((N_ATTN_LAYERS, KV_LORA, N_HEADS, QK_NOPE), KV_LORA ** -0.5)
    inp['mla_w_uv'] = nrm((N_ATTN_LAYERS, KV_LORA, N_HEADS, V_HEAD), KV_LORA ** -0.5)
    inp['mla_w_o'] = nrm((N_ATTN_LAYERS, N_HEADS * V_HEAD, d), (N_HEADS * V_HEAD) ** -0.5)
    inp['sgu_w_in'] = nrm((N_SGU_LAYERS, d, 2 * SGU_HALF), d ** -0.5)
    inp['sgu_b_in'] = nrm((N_SGU_LAYERS, 2 * SGU_HALF), 0.02)
    inp['sgu_g_v'] = gain((N_SGU_LAYERS, SGU_HALF))
    inp['sgu_b_v'] = nrm((N_SGU_LAYERS, SGU_HALF), 0.02)
    inp['sgu_w_s'] = nrm((N_SGU_LAYERS, SGU_GROUPS, SGU_CHUNK, SGU_CHUNK), SGU_CHUNK ** -0.5)
    inp['sgu_b_s'] = gain((N_SGU_LAYERS, SGU_GROUPS, SGU_CHUNK))
    inp['sgu_w_out'] = nrm((N_SGU_LAYERS, SGU_HALF, d), SGU_HALF ** -0.5)
    inp['moe_w_rg'] = nrm((DEPTH, d, N_EXPERT_GROUPS), d ** -0.5)
    inp['moe_b_rg'] = nrm((DEPTH, N_EXPERT_GROUPS), 0.01)
    inp['moe_w_re'] = nrm((DEPTH, d, N_EXPERTS), d ** -0.5)
    inp['moe_b_re'] = nrm((DEPTH, N_EXPERTS), 0.01)
    inp['moe_w_gate'] = nrm((DEPTH, N_EXPERTS, d, EXPERT_HIDDEN), d ** -0.5)
    inp['moe_w_up'] = nrm((DEPTH, N_EXPERTS, d, EXPERT_HIDDEN), d ** -0.5)
    inp['moe_w_down'] = nrm((DEPTH, N_EXPERTS, EXPERT_HIDDEN, d), EXPERT_HIDDEN ** -0.5)
    inp['ple_w_proj'] = nrm((DEPTH, PLE_DIM, d), PLE_DIM ** -0.5)
    inp['ple_w_gate'] = nrm((DEPTH, d, d), d ** -0.5)
    return inp

def reference(x_prompt, x_sample, cache_ckv, cache_krope, page_table, p_prompt, p_sample,
              g_mix, g_ffn, g_ple, g_final,
              mla_w_in, mla_g_q, mla_g_kv, mla_w_qb, mla_w_uk, mla_w_uv, mla_w_o,
              sgu_w_in, sgu_b_in, sgu_g_v, sgu_b_v, sgu_w_s, sgu_b_s, sgu_w_out,
              moe_w_rg, moe_b_rg, moe_w_re, moe_b_re, moe_w_gate, moe_w_up, moe_w_down,
              ple_w_proj, ple_w_gate):
    b_p, n_prompt = x_prompt.shape[0], x_prompt.shape[1]
    b_s, n_new = x_sample.shape[0], x_sample.shape[1]
    pos_p = jnp.arange(n_prompt, dtype=jnp.int32)
    pos_s = PAST_LEN + jnp.arange(n_new, dtype=jnp.int32)
    hp, hs = x_prompt, x_sample
    ckv_p_l, kr_p_l, ckv_s_l, kr_s_l, v_s_l = [], [], [], [], []
    for i in range(DEPTH):
        j = i // N_MIXERS
        hn_p = _rmsnorm(hp, g_mix[i])
        hn_s = _rmsnorm(hs, g_mix[i])
        if i % N_MIXERS == 0:
            wts = (mla_w_in[j], mla_g_q[j], mla_g_kv[j], mla_w_qb[j], mla_w_uk[j])
            ql, qr, c_p, r_p = _mla_project(hn_p, pos_p, *wts)
            o_p = _mla_prompt_attend(ql, qr, c_p, r_p)
            ql_s, qr_s, c_s, r_s = _mla_project(hn_s, pos_s, *wts)
            past_c = cache_ckv[j][page_table].reshape(b_s, -1, KV_LORA)
            past_r = cache_krope[j][page_table].reshape(b_s, -1, QK_ROPE)
            o_s = _mla_sample_attend(ql_s, qr_s, c_s, r_s, past_c, past_r)
            mix_p = _mla_output(o_p, mla_w_uv[j], mla_w_o[j])
            mix_s = _mla_output(o_s, mla_w_uv[j], mla_w_o[j])
            ckv_p_l.append(c_p)
            kr_p_l.append(r_p)
            ckv_s_l.append(c_s)
            kr_s_l.append(r_s)
        else:
            u_p, v_p = _sgu_project(hn_p, sgu_w_in[j], sgu_b_in[j], sgu_g_v[j], sgu_b_v[j])
            s_p = _spatial_gate(v_p.reshape(b_p, n_prompt // SGU_CHUNK, SGU_CHUNK, SGU_HALF),
                                sgu_w_s[j], sgu_b_s[j]).reshape(v_p.shape)
            mix_p = (u_p * s_p) @ sgu_w_out[j]
            u_s, v_s = _sgu_project(hn_s, sgu_w_in[j], sgu_b_in[j], sgu_g_v[j], sgu_b_v[j])
            s_s = _spatial_gate(v_s[:, None], sgu_w_s[j], sgu_b_s[j])[:, 0]
            mix_s = (u_s * s_s) @ sgu_w_out[j]
            v_s_l.append(v_s)
        hp = hp + mix_p
        hs = hs + mix_s
        moe_w = (moe_w_rg[i], moe_b_rg[i], moe_w_re[i], moe_b_re[i], moe_w_gate[i], moe_w_up[i], moe_w_down[i])
        hp = hp + _hier_moe(_rmsnorm(hp, g_ffn[i]), *moe_w)
        hs = hs + _hier_moe(_rmsnorm(hs, g_ffn[i]), *moe_w)
        hp = hp + _ple(hp, p_prompt[i], g_ple[i], ple_w_proj[i], ple_w_gate[i])
        hs = hs + _ple(hs, p_sample[i], g_ple[i], ple_w_proj[i], ple_w_gate[i])
    y_prompt = _rmsnorm(hp, g_final)
    y_sample = _rmsnorm(hs, g_final)
    ckv_prompt = jnp.stack(ckv_p_l)
    krope_prompt = jnp.stack(kr_p_l)
    ckv_sample = jnp.stack(ckv_s_l)
    krope_sample = jnp.stack(kr_s_l)
    sgu_v_sample = jnp.stack(v_s_l)
    return (y_prompt, y_sample, ckv_prompt, krope_prompt, ckv_sample, krope_sample, sgu_v_sample)


_drawn_inputs = setup_inputs


def setup_inputs(seed=0):
    import zlib

    import numpy as np

    out = dict(_drawn_inputs(seed))
    spreads = {}
    factors = {'g_ple': 31.786,
     'g_final': 8.556,
     'mla_g_q': 6.006,
     'mla_g_kv': 2.722,
     'sgu_g_v': 8.056,
     'sgu_b_v': 7.856,
     'moe_b_re': 3.441,
     'g_ffn': 2.82,
     'sgu_b_s': 7.97,
     'moe_b_rg': 4.73}
    for name, (base, spread) in spreads.items():
        noise = np.random.default_rng([zlib.crc32(name.encode()), seed]).standard_normal(out[name].shape)
        drawn = base * np.exp(spread * noise) if base else spread * noise
        out[name] = __import__('jax').numpy.asarray(drawn.astype(out[name].dtype))
    for name, factor in factors.items():
        out[name] = (out[name] * factor).astype(out[name].dtype)
    return out
```

```python
from contextlib import ExitStack

import numpy as np

import concourse.bass as bass
from concourse import mybir

FP = mybir.dt.float32
I32 = mybir.dt.int32
ACT = mybir.ActivationFunctionType
ALU = mybir.AluOpType
AX = mybir.AxisListType

P = 128
D, KD = 1024, 8
NP_, NS_ = 256, 32
T = NP_ + NS_
TOK = [(0, 128), (128, 128), (256, 32)]
H, DEC_B, DEC_S = 8, 8, 4
QL, KV, RO = 384, 256, 64
PAST, PAGE = 1024, 128
PAGES = PAST // PAGE
SCALE = (128 + 64) ** -0.5
FF, FT = 3072, 24
G, EPG, NE, FH = 4, 8, 32, 256
WIN = 64
PAIRS = NE // 2
PASSES = -(-T // WIN)
COLS = PASSES * PAIRS + 2
OOB = 9999.0
NEG = -1e30

SLOT, RING = 2048, 12
S_IN, S_QB, S_UK, S_UV, S_O = 0, 3, 6, 7, 8
S_PROJ = [12, 149]
S_MOE = [13, 150]
S_GATE = [109, 246]
S_SGU, S_OUT = 113, 137
N_SLOTS = 250

C_ID, C_ONE, C_LT, C_WM, C_WSM, C_IOTA, C_INV, C_TV = 0, 128, 256, 384, 512, 544, 552, 555
N_CONST = 567
C_MSK, C_SMSK, C_COS, C_SIN = 0, 384, 448, 736
N_ACONST = 1024
G_MIX, G_FFN, G_PLE, G_FIN, G_Q, G_KV = [0, 8], [16, 24], [32, 40], 48, 56, 59
B_IN, G_V, B_V = 61, 109, 133
N_PAR = 157

NORMS = [("mix0", 8), ("cq", 3), ("ckv", 2), ("ffn0", 8), ("ple0", 8), ("mix1", 8), ("ffn1", 8),
         ("ple1", 8), ("fin", 8)]
WO_BANK = (4, 5, 6, 0)
N_IDX = {name: n for n, (name, _) in enumerate(NORMS)}
N_BASE = {name: sum(k for _, k in NORMS[:n]) for n, (name, _) in enumerate(NORMS)}
N_K = dict(NORMS)
H_STAGE = {"mix0": 0, "ffn0": 1, "ple0": 2, "mix1": 3, "ffn1": 4, "ple1": 5, "fin": 6}


def slot_pos(s):
    return s % RING, s // RING + 1


def build(nc, io):
    with ExitStack() as ctx:
        program(nc, io, ctx)


def program(nc, io, ctx):
    made = {}

    def sem(name):
        if name not in made:
            made[name] = ctx.enter_context(nc.semaphore(name))
        return made[name]

    def sb(name, shape, dt=FP):
        return ctx.enter_context(nc.sbuf_tensor(name + "_sb", shape, dt))

    ring_t = sb("ring", [P, RING * SLOT])
    h_t = sb("h", [P, KD, T])
    hn_t = sb("hn", [P, KD, T])
    const = sb("const", [P, N_CONST])
    par = sb("par", [P, N_PAR])
    w_r = sb("w_r", [P, 2, KD, G + NE])
    b_r = sb("b_r", [P, 2, G + NE])
    eps = sb("eps", [P, 2])
    std_t = sb("std", [P, 2, T])
    rstd_t = sb("rstd", [P, 2, T])
    ptab = sb("ptab", [1, DEC_B * PAGES], I32)
    cnt_i = sb("cnt_i", [P, 2], I32)
    SCR = 21400
    scr = sb("scr", [P, SCR])
    ps = ctx.enter_context(nc.psum_tensor("ps", [P, 8, 512], FP))

    ident, ones = const[:, C_ID:C_ID + P], const[:, C_ONE:C_ONE + P]

    class Area:

        def __init__(self):
            self.at = 0

        def take(self, n, parts=P):
            a = scr[0:parts, self.at:self.at + n]
            self.at += n
            assert self.at <= SCR, self.at
            return a

    A = Area()
    aconst = A.take(N_ACONST)
    cq = A.take(3 * T).rearrange("p (k t) -> p k t", k=3)
    ckvT = A.take(2 * T).rearrange("p (k t) -> p k t", k=2)
    krT = A.take(T, RO)
    ckt = A.take(3 * KV).rearrange("p (t c) -> p t c", t=3)
    qn = A.take(H * T).rearrange("p (h t) -> p h t", h=H)
    ql = A.take(H * 2 * T).rearrange("p (h c t) -> p h c t", h=H, c=2)
    s_p = A.take(2 * 384).rearrange("p (b n) -> p b n", b=2)
    p_p = A.take(2 * 384).rearrange("p (b n) -> p b n", b=2)
    pt_p = A.take(384)
    p_s = A.take(PAST + NS_)
    pt_s = A.take(9 * P).rearrange("p (g r) -> p g r", g=9)
    ola_s = A.take(KV)
    snew = A.take(NS_)
    kv = A.take(2 * 4 * 2 * 384).rearrange("p (u b g n) -> p u b g n", u=2, b=4, g=2)
    rt = pt_s.rearrange("p g r -> p (g r)")[:, 0:2 * T].rearrange("p (a t) -> p a t", a=2)
    sm = A.take(32)
    qr = hn_t[0:RO, :, :]
    sq_a, sq_c = qn[:, 0:3, :], qn[:, 3:5, :]
    oT = qn
    qs = qn.rearrange("p h t -> p (h t)")[:, 0:3 * DEC_B * 32].rearrange("p (c b n) -> p c b n", c=3, b=DEC_B)
    mx, s_mx, s_nmx, s_l = sm[:, 0:2], sm[:, 2:4], sm[:, 4:5], sm[:, 5:7]
    nmx = sm[:, 8:12].rearrange("p (u n) -> p u n", u=2)
    lsum = sm[:, 12:16].rearrange("p (u n) -> p u n", u=2)
    rl = sm[:, 16:20].rearrange("p (u n) -> p u n", u=2)
    fill = p_s[0:COLS, 0:2 * P]

    M = Area()
    pT = M.take(2 * T).rearrange("p (k t) -> p k t", k=2)
    prj = M.take(KD * T).rearrange("p (k t) -> p k t", k=KD)
    x_sel = M.take(2 * D).rearrange("p (b n) -> p b n", b=2)
    xT = M.take(D).rearrange("p (k s) -> p k s", k=KD)
    sil = M.take(FH)
    act_a = M.take(FH)
    aT = M.take(2 * P).rearrange("p (k s) -> p k s", k=2)
    y_sb = M.take(2 * D).rearrange("p (b n) -> p b n", b=2)
    sg = M.take(4 * T).rearrange("p (b t) -> p b t", b=4)
    slots = M.take(2 * COLS).rearrange("p (c v) -> p c v", v=2).bitcast(I32)
    stage = M.take(4).rearrange("p (b v) -> p b v", b=2).bitcast(I32)
    gate_w = M.take(6).rearrange("p (t k) -> p t k", t=3)
    big0 = M.at
    big = M.take(5 * SLOT)
    hn_tok = big[:, 0:3 * D].rearrange("p (t n) -> p t n", t=3)
    tail_gu = big[:, 0:4 * SLOT].rearrange("p (a s n) -> p a s n", a=2, s=2)
    tail_dn = [big[:, 4 * SLOT:5 * SLOT], hn_t[:, :, :].rearrange("p k t -> p (k t)")[:, 0:SLOT]]
    y12 = big[:, 0:6 * D].rearrange("p (k t n) -> p k t n", k=2, t=3)
    R = Area()
    R.at = big0 + 3 * D
    lgt = R.take(3 * 36).rearrange("p (t n) -> p t n", t=3)
    lg, le = lgt[:, :, 0:G], lgt[:, :, G:G + NE].rearrange("p t (g j) -> p t g j", g=G)
    t4 = R.take(3 * G).rearrange("p (t g) -> p t g", t=3)
    t8 = R.take(3 * EPG).rearrange("p (t g) -> p t g", t=3)
    t32 = R.take(3 * NE).rearrange("p (t g j) -> p t g j", t=3, g=G)
    og = R.take(3 * G).rearrange("p (t g) -> p t g", t=3)
    leg = R.take(3 * EPG).rearrange("p (t j) -> p t j", t=3)
    leg2 = R.take(3 * EPG).rearrange("p (t j) -> p t j", t=3)
    oh = R.take(2 * 3 * EPG).rearrange("p (k t j) -> p k t j", k=2, t=3)
    ek = R.take(2 * 3 * NE).rearrange("p (k t e) -> p k t e", k=2, t=3)
    sel = R.take(3 * NE).rearrange("p (t e) -> p t e", t=3)
    gmx = R.take(3)
    gid = R.take(3)
    mk = R.take(6).rearrange("p (k t) -> p k t", k=2)
    ik = R.take(6).rearrange("p (k t) -> p k t", k=2)
    rk = R.take(6).rearrange("p (k t) -> p k t", k=2)
    win = R.take(6).rearrange("p (k t) -> p k t", k=2)
    row = R.take(6).rearrange("p (k t) -> p k t", k=2)
    row_i = R.take(6).rearrange("p (k t) -> p k t", k=2).bitcast(I32)
    dx = R.take(15)
    ex = R.take(15)
    gs = R.take(3)
    den = R.take(3)
    cmx = R.take(1)
    lst = R.take(2 * P, COLS)

    U = Area()
    uT = U.take(FT * T).rearrange("p (f t) -> p f t", f=FT)
    v_tok = U.take(3 * FF).rearrange("p (t f) -> p t f", t=3)
    vT = U.take(2 * T).rearrange("p (b t) -> p b t", b=2)
    wsT = U.take(G * 2 * P).rearrange("p (g r) -> p g r", g=8)
    wsS = U.take(8 * NS_, NS_).rearrange("p (g r) -> p g r", g=8)
    rs = U.take(8 * 160).rearrange("p (g r) -> p g r", g=8)
    bs = U.take(8 * 160).rearrange("p (g r) -> p g r", g=8)
    tm = U.take(T)
    sr = U.take(T)
    bst = U.take(3 * 36)
    mv = U.take(6).rearrange("p (t v) -> p t v", t=3)
    vst = U.take(6).rearrange("p (t v) -> p t v", t=3)
    vsT = hn_t[:, :, :].rearrange("p k t -> p (k t)")[:, 0:FT * NS_].rearrange("p (f t) -> p f t", f=FT)

    lists, hn_rows, y_rows = io["lists"], io["hn_rows"], io["y_rows"]

    def bank(b, n=512):
        return ps[:, b, 0:n]

    def ring(s, at, n):
        o = (s % RING) * SLOT + at
        assert o + n <= RING * SLOT
        return ring_t[:, o:o + n]

    owed = [0]

    def owe(n):
        owed[0] += n

    def free_with(ins):
        if owed[0]:
            ins.then_inc(sem("slot_free"), owed[0])
            owed[0] = 0
        return ins

    def wait_slots(pe, s0, s1):
        for s in range(s0, s1):
            pos, n = slot_pos(s)
            pe.wait_ge(sem(f"slot_full{pos}"), 16 * n)

    block = ctx.enter_context(nc.Block())

    @block.sync
    def _(sp):
        stream = io["stream"]

        def load_slot(s):
            pos, _ = slot_pos(s)
            if s >= RING:
                sp.wait_ge(sem("slot_free"), s - RING + 1)
            sp.dma_start(ring(pos, 0, SLOT), stream[s]).then_inc(sem(f"slot_full{pos}"), 16)

        def load_pages(rnd, kind, cc, u):
            sp.wait_ge(sem("kv_free"), cc * 2 + (8 * rnd + 4 * kind + u + 1))
            for b in range(4):
                for pg in range(2):
                    at = (4 * rnd + b) * PAGES + 2 * u + pg
                    page = sp.value_load(ptab[0:1, bass.ds(cc * 4 + at, 1)], min_val=0,
                                         max_val=io["n_phys"] - 1)
                    if kind == 0:
                        sp.dma_start(kv[:, u, b, pg, 0:256],
                                     io["ckv_t"][bass.ds(page, 1)].rearrange("a p n -> (a p) n")
                                     ).then_inc(sem(f"kv_full{u}"), 16)
                        sp.dma_start(kv[0:RO, u, b, pg, 256:384],
                                     io["kr_t"][bass.ds(page, 1)].rearrange("a p n -> (a p) n")
                                     ).then_inc(sem(f"kv_full{u}"), 16)
                    else:
                        sp.dma_start(kv[:, u, b, pg, 0:256],
                                     io["ckv_n"][bass.ds(page, 1)].rearrange("a p n -> (a p) n")
                                     ).then_inc(sem(f"kv_full{u}"), 16)

        sp.dma_start(h_t[:, :, :], io["x"]).then_inc(sem("x_in"), 16)
        for s in range(RING):
            load_slot(s)
        sp.wait_ge(sem("ptab_in"), 16)
        load_pages(0, 0, 0, 0)
        load_pages(0, 0, 0, 1)
        for s in range(RING, RING + 7):
            load_slot(s)
        load_pages(0, 0, 1, 0)
        load_pages(0, 0, 1, 1)
        for rnd, kind in ((0, 1), (1, 0), (1, 1)):
            with sp.Fori(0, 2) as cc:
                for u in range(2):
                    load_pages(rnd, kind, cc, u)
        for s in range(RING + 7, 2 * RING):
            load_slot(s)
        with sp.Fori(2, N_SLOTS // RING) as i:
            for j in range(RING):
                sp.wait_ge(sem("slot_free"), i * RING + (j + 1 - RING))
                sp.dma_start(ring(j, 0, SLOT), stream[bass.ds(i * RING + j, 1)].rearrange("a p n -> (a p) n")
                             ).then_inc(sem(f"slot_full{j}"), 16)
        for s in range(N_SLOTS // RING * RING, N_SLOTS):
            load_slot(s)

    @block.gpsimd
    def _(pool):
        def moe(L):
            pool.wait_ge(sem("h_upd"), 8 * (1 if L == 0 else 4))
            pool.memset(x_sel, 0.0).then_inc(sem("x_clear"), 1)
            pool.wait_ge(sem("list_clear"), 32)
            pool.wait_ge(sem("row_i"), L + 1)
            for k in range(2):
                for t in range(3):
                    pool.indirect_dma_start(
                        out=lists[L], out_offset=bass.IndirectOffsetOnAxis(ap=row_i[:, k, t:t + 1], axis=0),
                        in_=const[:, C_TV + 4 * t + 2 * k:C_TV + 4 * t + 2 * k + 2], in_offset=None,
                        bounds_check=COLS * P - 1, oob_is_err=False).then_inc(sem("list_put"), 16)
            pool.wait_ge(sem("list_put"), 96 * L + 6 * 16)
            pool.dma_start(lst[:, :], lists[L].rearrange("(c r) v -> c (r v)", r=P)).then_inc(sem("list_in"), 16)
            pool.wait_ge(sem("slots"), L + 1)
            pool.wait_ge(sem("hn_rows"), 48 * L + 3 * 16)
            pool.wait_ge(sem("x_clear"), L + 1)
            pool.sem_inc(sem(f"y_free{L}"), 2)

            def gather(col, b, n_staged):
                pool.tensor_copy(stage[:, b, :], col).then_inc(sem(f"staged{L}"), 1)
                pool.wait_ge(sem(f"staged{L}"), n_staged)
                pool.sem_inc(sem("pool_step"), 1)
                pool.indirect_dma_start(
                    out=x_sel[:, b, :], out_offset=None, in_=hn_rows[L],
                    in_offset=bass.IndirectOffsetOnAxis(ap=stage[:, b, 0:1], axis=0),
                    bounds_check=T - 1, oob_is_err=False).then_inc(sem(f"x_got{L}_{b}"), 16)

            def pair(i, b, tail=None):
                if tail is not None:
                    pool.wait_ge(sem(f"y_ps{L}"), i * 2 + b)
                    w0 = S_MOE[L] + 6 * b
                    for a in range(2):
                        pool.dma_start(tail_gu[:, a, :, :], io["stream"][bass.ds(tail * 12 + (w0 + 2 * a), 2)]
                                       .rearrange("s p n -> p s n")).then_inc(sem(f"tail_w{L}"), 16)
                        pool.dma_start(tail_dn[a], io["stream"][bass.ds(tail * 12 + (w0 + 4 + a), 1)]
                                       .rearrange("s p n -> (s p) n")).then_inc(sem(f"tail_w{L}"), 16)
                pool.wait_ge(sem(f"y_a{L}"), i * 2 + (b + 2))
                pool.wait_ge(sem(f"y_d{L}"), i * 2 + (b + 2))
                pool.sem_inc(sem("pool_step"), 1)
                pool.indirect_dma_start(
                    out=y_rows[L], out_offset=bass.IndirectOffsetOnAxis(ap=stage[:, b, 1:2], axis=0),
                    in_=y_sb[:, b, :], in_offset=None,
                    bounds_check=2 * T - 1, oob_is_err=False).then_inc(sem(f"y_put{L}_{b}"), 16)
                pool.wait_ge(sem(f"y_put{L}_{b}"), i * 16 + 16)
                pool.wait_ge(sem(f"x_got{L}_{b}"), i * 16 + 16)
                pool.wait_ge(sem(f"x_ps{L}"), i * 2 + (b + 1))
                pool.sem_inc(sem(f"y_free{L}"), 1)
                gather(slots[:, bass.ds(i * 2 + (b + 2), 1), :].rearrange("p c v -> p (c v)"), b,
                       i * 2 + (b + 3))

            for b in range(2):
                gather(slots[:, b, :], b, b + 1)
            with pool.Fori(0, PAIRS // 2) as i:
                for b in range(2):
                    pair(i, b)
            pool.wait_ge(sem("cnt"), L + 1)
            most = pool.value_load(cnt_i[0:1, L:L + 1], min_val=0, max_val=T)
            with pool.If(most > WIN):
                with pool.Fori(0, PASSES - 1) as p:
                    with pool.Fori(0, PAIRS // 2) as q:
                        for b in range(2):
                            pair(p * (PAIRS // 2) + q + PAIRS // 2, b, q)
                for b in range(2):
                    pool.wait_ge(sem(f"x_got{L}_{b}"), 16 * (PASSES * PAIRS // 2 + 1))
            for b in range(2):
                pool.wait_ge(sem(f"x_got{L}_{b}"), 16 * (PAIRS // 2 + 1))
            for k in range(2):
                pool.dma_start(y12[:, k, 0:2, :], y_rows[L][k * T:k * T + 256, :]
                               .rearrange("(t p) n -> p t n", p=P)).then_inc(sem("y12_in"), 16)
                pool.dma_start(y12[0:NS_, k, 2, :], y_rows[L][k * T + 256:k * T + T, :]
                               ).then_inc(sem("y12_in"), 16)

        pool.memset(fill[:, :], OOB).then_inc(sem("fill"), 1)
        pool.wait_ge(sem("fill"), 1)
        for L in range(2):
            pool.dma_start(lists[L].rearrange("(c r) v -> c (r v)", r=P), fill[:, :]
                           ).then_inc(sem("list_clear"), 16)
        moe(0)
        moe(1)

    @block.scalar
    def _(act):
        def norm(name, src, sq, feats):
            n = N_IDX[name]
            for k in range(N_K[name]):
                if name in H_STAGE and H_STAGE[name]:
                    act.wait_ge(sem("h_upd"), 8 * (H_STAGE[name] - 1) + k + 1)
                nc.scalar.activation(sq[:, k, :], src[:, k, :], ACT.Square).then_inc(sem("sq"), 1)
            act.wait_ge(sem("ss_ps"), n + 1)
            if n >= 2:
                act.wait_ge(sem("rstd"), n - 1)
            nc.scalar.activation(std_t[:, n % 2, :], bank(7, T), ACT.Sqrt, bias=eps[:, 0:1],
                                 scale=1.0 / feats).then_inc(sem("std"), 1)

        act.dma_start(par[:, :], io["par"]).then_inc(sem("par_in"), 16)
        act.dma_start(const[:, :], io["const"]).then_inc(sem("const_in"), 16)
        act.dma_start(aconst, io["aconst"]).then_inc(sem("aconst_in"), 16)
        act.dma_start(ptab[:, :], io["ptab"]).then_inc(sem("ptab_in"), 16)
        act.dma_start(w_r[:, :, :, :], io["w_r"]).then_inc(sem("wr_in"), 16)
        act.dma_start(b_r[:, :, :], io["b_r"]).then_inc(sem("wr_in"), 16)

        act.wait_ge(sem("x_in"), 16)
        act.wait_ge(sem("eps"), 2)
        norm("mix0", h_t, hn_t, D)
        for m in range(5):
            act.wait_ge(sem("a_ps"), m + 1)
            dst = cq[:, m, :] if m < 3 else ckvT[:, m - 3, :]
            nc.scalar.activation(dst, bank(m, T), ACT.Copy).then_inc(sem("a_sb"), 1)
        act.wait_ge(sem("a_sb"), 5)
        norm("cq", cq, sq_a, QL)
        norm("ckv", ckvT, sq_c, KV)
        act.wait_ge(sem("hn"), N_BASE["ckv"] + 2)
        act.dma_start(io["ckv_out"], ckvT[:, :, :]).then_inc(sem("out"), 16)
        act.wait_ge(sem("kr"), 1)
        act.dma_start(io["kr_out"], krT).then_inc(sem("out"), 16)
        for h in range(H):
            act.wait_ge(sem("qn_ps"), h + 1)
            nc.scalar.activation(qn[:, h, :], bank(2 + h % 2, T), ACT.Copy).then_inc(sem("qn_sb"), 1)
        for h in range(H):
            act.wait_ge(sem("ql_ps"), 2 * h + 1)
            nc.scalar.activation(ql[:, h, 0, :], bank((2 * h) % 4, T), ACT.Copy).then_inc(sem("ql_a"), 1)

        def exp_prompt(h):
            u = h % 2
            act.wait_ge(sem("nmax"), h + 1)
            if h >= 2:
                act.wait_ge(sem("pt_ps"), h - 1)
            nc.scalar.activation(p_p[:, u, 0:128], s_p[:, u, 0:128], ACT.Exp, bias=nmx[:, u, 0:1],
                                 scale=SCALE, accum_out=lsum[:, u, 0:1])
            nc.scalar.activation(p_p[:, u, 128:384], s_p[:, u, 128:384], ACT.Exp, bias=nmx[:, u, 1:2],
                                 scale=SCALE, accum_out=lsum[:, u, 1:2]).then_inc(sem("exp"), 1)

        def copy_pt(h):
            act.wait_ge(sem("pt_ps"), h + 1)
            nc.scalar.activation(pt_p[:, :], bank(2, 384), ACT.Copy).then_inc(sem("pt_sb"), 1)

        def exp_sample(r):
            act.wait_ge(sem("s_nmax"), r + 1)
            if r == 0:
                act.wait_ge(sem("list_clear"), 32)
            nc.scalar.activation(p_s[:, 0:PAST].rearrange("p (b n) -> p b n", b=2), ps[:, 4:6, :], ACT.Exp, bias=s_nmx,
                                 scale=SCALE, accum_out=s_l[:, 0:1])
            nc.scalar.activation(p_s[:, PAST:PAST + NS_], snew, ACT.Exp, bias=s_nmx, scale=SCALE,
                                 accum_out=s_l[:, 1:2]).then_inc(sem("s_exp"), 1)

        def copy_pts(r):
            act.wait_ge(sem("s_pt_ps"), r + 1)
            nc.scalar.activation(pt_s[:, 0:4, :].rearrange("p g r -> p (g r)"), bank(4), ACT.Copy
                                 ).then_inc(sem("s_pt_a"), 1)

        exp_prompt(0)
        for h in range(H):
            if h + 1 < H:
                exp_prompt(h + 1)
            if h in (2, 6):
                exp_sample(h // 4)
            if h == 3:
                copy_pts(0)
            copy_pt(h)
        copy_pts(1)
        for h in range(0, H, 2):
            act.wait_ge(sem("o_ps"), h + 1)
            nc.scalar.activation(oT[:, h, :], bank(h % 4, T), ACT.Copy).then_inc(sem("o_a"), 1)

        def moe(L):
            if L == 0:
                act.wait_ge(sem("out"), 32)
            norm(f"ffn{L}", h_t, hn_t, D)
            act.wait_ge(sem("h_upd"), 8 * (1 if L == 0 else 4))
            act.dma_start(pT, io["p"][:, L]).then_inc(sem("pT_in"), 16)
            for t, (t0, tn) in enumerate(TOK):
                act.wait_ge(sem("hr_ps"), 3 * L + t + 1)
                if t == 2:
                    act.wait_ge(sem("hr_d"), 3 * L + 1)
                nc.scalar.activation(hn_tok[0:tn, t, 0:512], ps[0:tn, 2 + 2 * (t % 2), :], ACT.Copy).then_inc(sem("hr_a"), 1)
                act.wait_ge(sem("hr_a"), 3 * L + t + 1)
                act.wait_ge(sem("hr_d"), 3 * L + t + 1)
                act.dma_start(hn_rows[L][t0:t0 + tn, :], hn_tok[0:tn, t, :]).then_inc(sem("hn_rows"), 16)
            act.wait_ge(sem("dx"), L + 1)
            nc.scalar.activation(ex, dx, ACT.Exp).then_inc(sem("ex"), 1)
            for m in range(KD):
                act.wait_ge(sem("prj_ps"), 8 * L + m + 1)
                nc.scalar.activation(prj[:, m, :], bank(4 + m % 4, T), ACT.Copy).then_inc(sem("prj"), 1)

            def pair(i, b):
                act.wait_ge(sem(f"x_ps{L}"), i * 2 + (b + 1))
                nc.scalar.activation(xT[:, 0:4, :].rearrange("p k s -> p (k s)"), bank(0), ACT.Copy).then_inc(sem(f"xT_a{L}"), 1)
                act.wait_ge(sem(f"h_ps{L}"), i * 2 + (b + 1))
                nc.scalar.activation(sil, ps[:, 2 + b, 0:FH], ACT.Silu).then_inc(sem(f"sil{L}"), 1)
                act.wait_ge(sem(f"aT_ps{L}"), i * 2 + (b + 1))
                nc.scalar.activation(aT.rearrange("p k s -> p (k s)"), ps[:, 4, 0:256], ACT.Copy).then_inc(sem(f"aT{L}"), 1)
                act.wait_ge(sem(f"y_ps{L}"), i * 2 + (b + 1))
                act.wait_ge(sem(f"y_free{L}"), i * 2 + (b + 1))
                nc.scalar.activation(y_sb[:, b, 0:512], bank(5), ACT.Copy).then_inc(sem(f"y_a{L}"), 1)

            act.sem_inc(sem(f"y_a{L}"), 1)
            with act.Fori(0, PAIRS // 2) as i:
                for b in range(2):
                    pair(i, b)
            act.wait_ge(sem("cnt"), L + 1)
            most = act.value_load(cnt_i[0:1, L:L + 1], min_val=0, max_val=T)
            with act.If(most > WIN):
                with act.Fori(PAIRS // 2, PASSES * PAIRS // 2) as i:
                    for b in range(2):
                        pair(i, b)
            norm(f"ple{L}", h_t, hn_t, D)
            for m in range(KD):
                act.wait_ge(sem("pg_ps"), 8 * L + m + 1)
                if m >= 4:
                    act.wait_ge(sem("h_upd"), 8 * (2 if L == 0 else 5) + m - 3)
                nc.scalar.activation(sg[:, m % 4, :], bank(m % 4, T), ACT.Sigmoid).then_inc(sem("pg_sig"), 1)

        moe(0)

        act.wait_ge(sem("h_upd"), 24)
        for name, dst in (("ws", wsT), ("wss", wsS), ("bs", bs)):
            act.dma_start(dst, io[name]).then_inc(sem("ws_in"), 16)
        norm("mix1", h_t, hn_t, D)
        for t in range(FT):
            act.wait_ge(sem("z_ps"), t + 1)
            if t >= 2:
                act.wait_ge(sem("vt_ps"), t - 1)
            nc.scalar.activation(vT[:, t % 2, :], bank(t % 4, T), ACT.Gelu_apprx_tanh,
                                 bias=par[:, B_IN + FT + t:B_IN + FT + t + 1]).then_inc(sem("z_sb"), 1)
        for t in range(FT):
            if t == 3:
                act.wait_ge(sem("v_mv"), 3)
                act.wait_ge(sem("vst_init"), 1)
                nc.scalar.activation(vst[:, 0:2, 0:1], mv[:, 0:2, 1:2], ACT.Sqrt, bias=eps[:, 1:2]).then_inc(sem("v_std"), 1)
                nc.scalar.activation(vst[0:NS_, 2, 0:1], mv[0:NS_, 2, 1:2], ACT.Sqrt, bias=eps[0:NS_, 1:2]).then_inc(sem("v_std"), 1)
            act.wait_ge(sem("z_ps"), FT + t + 1)
            nc.scalar.activation(uT[:, t, :], bank(t % 4, T), ACT.Gelu_apprx_tanh,
                                 bias=par[:, B_IN + t:B_IN + t + 1]).then_inc(sem("z_sb"), 1)
        act.wait_ge(sem("vs"), 1)
        act.dma_start(io["vs_out"], vsT).then_inc(sem("vs_out"), 16)
        act.wait_ge(sem("vs_out"), 16)
        moe(1)
        norm("fin", h_t, hn_t, D)
        for k in range(KD):
            act.wait_ge(sem("hn"), N_BASE["fin"] + k + 1)
            act.dma_start(io["y_out"][:, k, :], hn_t[:, k, :]).then_inc(sem("out"), 16)
        act.wait_ge(sem("out"), 16 * (2 + KD))

    @block.vector
    def _(dve):
        done = [0]

        def link(ins):
            done[0] += 1
            ins.then_inc(sem("dve_step"), 1)
            dve.wait_ge(sem("dve_step"), done[0])

        def norm(name, src, dst, g0):
            n = N_IDX[name]
            dve.wait_ge(sem("std"), n + 1)
            nc.vector.reciprocal(rstd_t[:, n % 2, :], std_t[:, n % 2, :]).then_inc(sem("rstd"), 1)
            dve.wait_ge(sem("rstd"), n + 1)
            for k in range(N_K[name]):
                nc.vector.scalar_tensor_tensor(out=dst[:, k, :], in0=src[:, k, :],
                                               scalar=par[:, g0 + k:g0 + k + 1], in1=rstd_t[:, n % 2, :],
                                               op0=ALU.mult, op1=ALU.mult).then_inc(sem("hn"), 1)

        def add_h(k, what):
            nc.vector.tensor_tensor(h_t[:, k, :], h_t[:, k, :], what, ALU.add).then_inc(sem("h_upd"), 1)

        nc.vector.memset(eps[:, 0:1], 1e-6).then_inc(sem("eps"), 1)
        nc.vector.memset(eps[:, 1:2], 1e-5).then_inc(sem("eps"), 1)
        dve.wait_ge(sem("par_in"), 16)
        dve.wait_ge(sem("const_in"), 16)
        norm("mix0", h_t, hn_t, G_MIX[0])

        dve.wait_ge(sem("aconst_in"), 16)
        cos, sin = aconst[:, C_COS:C_COS + T], aconst[:, C_SIN:C_SIN + T]
        norm("cq", cq, cq, G_Q)
        norm("ckv", ckvT, ckvT, G_KV)
        dve.wait_ge(sem("a_ps"), 7)
        nc.vector.tensor_tensor(rt[0:RO, 0, :], ps[0:RO, 5, 0:T], cos[0:RO], ALU.mult).then_inc(sem("kr_t"), 1)
        nc.vector.tensor_tensor(rt[0:RO, 1, :], ps[0:RO, 6, 0:T], sin[0:RO], ALU.mult).then_inc(sem("kr_t"), 1)
        dve.wait_ge(sem("kr_t"), 2)
        nc.vector.tensor_tensor(krT, rt[0:RO, 0, :], rt[0:RO, 1, :], ALU.add).then_inc(sem("kr"), 1)
        dve.wait_ge(sem("kr"), 1)
        dve.wait_ge(sem("ckt_ps"), 1)
        nc.vector.tensor_copy(ckt[:, 0:2, :].rearrange("p t c -> p (t c)"), bank(0)).then_inc(sem("ckt"), 1)
        nc.vector.tensor_copy(ckt[0:NS_, 2, :], ps[0:NS_, 1, 0:KV]).then_inc(sem("ckt"), 1)
        for p in range(H // 2):
            b0 = 4 + 2 * (p % 2)
            dve.wait_ge(sem("qr_ps"), p + 1)
            link(nc.vector.tensor_tensor(rt[:, 0, :], bank(b0, T), cos, ALU.mult))
            link(nc.vector.tensor_tensor(rt[:, 1, :], bank(b0 + 1, T), sin, ALU.mult))
            link(nc.vector.tensor_tensor(qr[:, 2 * p, :], rt[0:RO, 0, :], rt[0:RO, 1, :], ALU.add))
            nc.vector.tensor_tensor(qr[:, 2 * p + 1, :], rt[RO:P, 0, :], rt[RO:P, 1, :], ALU.add).then_inc(sem("qr"), 1)
            dve.wait_ge(sem("qr"), p + 1)
        for h in range(H):
            dve.wait_ge(sem("ql_ps"), 2 * h + 2)
            nc.vector.tensor_copy(ql[:, h, 1, :], bank((2 * h + 1) % 4, T)).then_inc(sem("ql_d"), 1)

        dve.wait_ge(sem("ql_a"), H)
        dve.wait_ge(sem("ql_d"), H)
        for c in range(3):
            a, n = (ql[:, :, c, NP_:T], P) if c < 2 else (qr[:, :, NP_:T], RO)
            nc.vector.tensor_copy(qs[0:n, c].rearrange("p b (h s) -> p b h s", h=H),
                                  a.rearrange("p h (b s) -> p b h s", b=DEC_B)).then_inc(sem("qs"), 1)

        def max_prompt(h):
            u = h % 2
            dve.wait_ge(sem("sc_ps"), h + 1)
            nc.vector.tensor_tensor(s_p[:, u, :], bank(u, 384), aconst[:, C_MSK:C_MSK + 384], ALU.add).then_inc(sem("masked"), 1)
            dve.wait_ge(sem("masked"), h + 1)
            link(nc.vector.tensor_reduce(mx[:, 0:1], s_p[:, u, 0:128], AX.X, ALU.max))
            link(nc.vector.tensor_reduce(mx[:, 1:2], s_p[:, u, 128:384], AX.X, ALU.max))
            nc.vector.tensor_scalar(nmx[:, u, :], mx, -SCALE, None, ALU.mult).then_inc(sem("nmax"), 1)

        def norm_prompt(h):
            u = h % 2
            dve.wait_ge(sem("exp"), h + 1)
            link(nc.vector.reciprocal(rl[:, u, :], lsum[:, u, :]))
            link(nc.vector.tensor_scalar(p_p[:, u, 0:128], p_p[:, u, 0:128], rl[:, u, 0:1], None, ALU.mult))
            nc.vector.tensor_scalar(p_p[:, u, 128:384], p_p[:, u, 128:384], rl[:, u, 1:2], None, ALU.mult).then_inc(sem("p_n"), 1)

        def take_prompt(h):
            dve.wait_ge(sem("pv_ps"), h + 1)
            nc.vector.tensor_copy(ql[:, h, :, 0:NP_], ps[:, 3, :].rearrange("p (c t) -> p c t", c=2)).then_inc(sem("ol"), 1)

        def max_sample(r):
            dve.wait_ge(sem("s_ps"), r + 1)
            link(nc.vector.tensor_tensor(snew, ps[:, 6, 0:NS_], aconst[:, C_SMSK + NS_ * r:C_SMSK + NS_ * r + NS_], ALU.add))
            link(nc.vector.tensor_reduce(s_mx[:, 0:1], ps[:, 4:6, :], AX.XY, ALU.max))
            link(nc.vector.tensor_reduce(s_mx[:, 1:2], snew, AX.X, ALU.max))
            link(nc.vector.tensor_tensor(s_mx[:, 0:1], s_mx[:, 0:1], s_mx[:, 1:2], ALU.max))
            nc.vector.tensor_scalar(s_nmx, s_mx[:, 0:1], -SCALE, None, ALU.mult).then_inc(sem("s_nmax"), 1)

        def norm_sample(r):
            dve.wait_ge(sem("s_exp"), r + 1)
            link(nc.vector.tensor_tensor(s_l[:, 0:1], s_l[:, 0:1], s_l[:, 1:2], ALU.add))
            link(nc.vector.reciprocal(s_l[:, 1:2], s_l[:, 0:1]))
            nc.vector.tensor_scalar(p_s, p_s, s_l[:, 1:2], None, ALU.mult).then_inc(sem("s_pn"), 1)

        def take_pts(r):
            dve.wait_ge(sem("s_pt_ps"), r + 1)
            nc.vector.tensor_copy(pt_s[:, 4:8, :].rearrange("p g r -> p (g r)"), bank(5)).then_inc(sem("s_pt_d"), 1)
            nc.vector.tensor_copy(pt_s[0:NS_, 8, :], ps[0:NS_, 6, 0:P]).then_inc(sem("s_pt_d"), 1)

        def take_ola(r):
            dve.wait_ge(sem("s_o_ps"), r + 1)
            nc.vector.tensor_copy(ola_s, bank(7, KV)).then_inc(sem("s_ola"), 1)

        def take_ol(r):
            dve.wait_ge(sem("s_ot_ps"), r + 1)
            for c in range(2):
                nc.vector.tensor_copy(
                    ql[:, :, c, NP_ + 16 * r:NP_ + 16 * r + 16].rearrange("p h (b s) -> p b h s", b=4),
                    ps[:, 6, 128 + 128 * c:256 + 128 * c].rearrange("p (b h s) -> p b h s", b=4, h=H)
                ).then_inc(sem("s_ol"), 1)

        max_prompt(0)
        for h in range(H):
            if h + 1 < H:
                max_prompt(h + 1)
            if h == 3:
                take_pts(0)
            norm_prompt(h)
            if h in (1, 5):
                max_sample(h // 4)
            if h in (2, 6):
                norm_sample(h // 4)
            take_prompt(h)
            if h == 4:
                take_ola(0)
                take_ol(0)
        take_pts(1)
        take_ola(1)
        take_ol(1)
        for h in range(1, H, 2):
            dve.wait_ge(sem("o_ps"), h + 1)
            nc.vector.tensor_copy(oT[:, h, :], bank(h % 4, T)).then_inc(sem("o_d"), 1)
        for m in range(KD):
            dve.wait_ge(sem("wo_ps"), m + 1)
            add_h(m, bank(WO_BANK[m % 4], T))

        io3 = const[:, C_IOTA:C_IOTA + EPG]

        def bc(a, shape):
            return a.to_broadcast(shape)

        def first_of(vals, top, n, tmp, out):
            link(nc.vector.tensor_tensor(tmp, vals, bc(top.unsqueeze(2), [P, 3, n]), ALU.is_lt))
            link(nc.vector.scalar_tensor_tensor(out=tmp, in0=tmp, scalar=100.0,
                                                in1=bc(io3[:, 0:n].unsqueeze(1), [P, 3, n]),
                                                op0=ALU.mult, op1=ALU.add))
            link(nc.vector.tensor_reduce(out, tmp, AX.X, ALU.min))

        def moe(L):
            norm(f"ffn{L}", h_t, hn_t, G_FFN[L])
            for t, (t0, tn) in enumerate(TOK):
                dve.wait_ge(sem("hr_ps"), 3 * L + t + 1)
                nc.vector.tensor_copy(hn_tok[0:tn, t, 512:1024], ps[0:tn, 3 + 2 * (t % 2), :]).then_inc(sem("hr_d"), 1)
            dve.wait_ge(sem("wr_in"), 32)
            link(nc.vector.memset(lgt[:, 2, :], 0.0))
            dve.wait_ge(sem("lg_ps"), L + 1)
            pl = ps[:, 0, 0:108].rearrange("p (t n) -> p t n", t=3)
            link(nc.vector.tensor_tensor(lgt[:, 0:2, :], pl[:, 0:2, :], bc(b_r[:, L, :].unsqueeze(1), [P, 2, 36]), ALU.add))
            link(nc.vector.tensor_tensor(lgt[0:NS_, 2, :], pl[0:NS_, 2, :], b_r[0:NS_, L, :], ALU.add))
            link(nc.vector.tensor_reduce(gmx, lg, AX.X, ALU.max))
            dx4 = dx[:, 0:12].rearrange("p (t g) -> p t g", t=3)
            link(nc.vector.tensor_tensor(dx4, lg, bc(gmx.unsqueeze(2), [P, 3, G]), ALU.subtract))
            first_of(lg, gmx, G, t4, gid)
            link(nc.vector.tensor_tensor(og, bc(io3[:, 0:G].unsqueeze(1), [P, 3, G]), bc(gid.unsqueeze(2), [P, 3, G]), ALU.is_equal))
            link(nc.vector.tensor_tensor(t32, le, bc(og.unsqueeze(3), [P, 3, G, EPG]), ALU.mult))
            link(nc.vector.tensor_reduce(leg, t32.rearrange("p t g j -> p t j g"), AX.X, ALU.add))
            for k, src in ((0, leg), (1, leg2)):
                link(nc.vector.tensor_reduce(mk[:, k, :], src, AX.X, ALU.max))
                first_of(src, mk[:, k, :], EPG, t8, ik[:, k, :])
                link(nc.vector.tensor_tensor(oh[:, k], bc(io3.unsqueeze(1), [P, 3, EPG]), bc(ik[:, k, :].unsqueeze(2), [P, 3, EPG]), ALU.is_equal))
                if k == 0:
                    link(nc.vector.scalar_tensor_tensor(out=leg2, in0=oh[:, 0], scalar=NEG, in1=leg, op0=ALU.mult, op1=ALU.add))
                link(nc.vector.tensor_tensor(ek[:, k].rearrange("p t (g j) -> p t g j", g=G),
                                             bc(og.unsqueeze(3), [P, 3, G, EPG]),
                                             bc(oh[:, k].unsqueeze(2), [P, 3, G, EPG]), ALU.mult))
            nc.vector.tensor_tensor(sel, ek[:, 0], ek[:, 1], ALU.add).then_inc(sem("sel"), 1)
            nc.vector.tensor_tensor(dx[:, 12:15], mk[:, 1, :], mk[:, 0, :], ALU.subtract).then_inc(sem("dx"), 1)
            dve.wait_ge(sem("ex"), L + 1)
            link(nc.vector.tensor_reduce(gs, ex[:, 0:12].rearrange("p (t g) -> p t g", t=3), AX.X, ALU.add))
            link(nc.vector.tensor_scalar(den, ex[:, 12:15], 1.0, None, ALU.add))
            link(nc.vector.tensor_tensor(den, den, gs, ALU.mult))
            link(nc.vector.reciprocal(gate_w[:, :, 0], den))
            link(nc.vector.tensor_tensor(gate_w[:, :, 1], gate_w[:, :, 0], ex[:, 12:15], ALU.mult))
            dve.wait_ge(sem("rank_ps"), L + 1)
            link(nc.vector.tensor_reduce(cmx, ps[:, 1, 96:128], AX.X, ALU.max))
            nc.vector.tensor_copy(cnt_i[:, L:L + 1], cmx).then_inc(sem("cnt"), 1)
            t32f = t32.rearrange("p t g j -> p t (g j)")
            for k in range(2):
                link(nc.vector.tensor_tensor(t32f, ek[:, k], ps[:, 1, 0:96].rearrange("p (t e) -> p t e", t=3), ALU.mult))
                link(nc.vector.tensor_reduce(rk[:, k, :], t32f, AX.X, ALU.add))
            link(nc.vector.tensor_scalar(win, rk, float(WIN), None, ALU.is_ge))
            for j in range(2, PASSES):
                link(nc.vector.scalar_tensor_tensor(out=win, in0=rk, scalar=float(WIN * j), in1=win, op0=ALU.is_ge, op1=ALU.add))
            link(nc.vector.scalar_tensor_tensor(out=row, in0=win, scalar=float(WIN * NE - WIN), in1=rk, op0=ALU.mult, op1=ALU.add))
            link(nc.vector.scalar_tensor_tensor(out=row, in0=ik, scalar=float(WIN), in1=row, op0=ALU.mult, op1=ALU.add))
            link(nc.vector.scalar_tensor_tensor(out=row, in0=bc(gid.unsqueeze(1), [P, 2, 3]), scalar=float(WIN * EPG), in1=row, op0=ALU.mult, op1=ALU.add))
            link(nc.vector.tensor_tensor(row, row, bc(const[:, C_INV:C_INV + 3].unsqueeze(1), [P, 2, 3]), ALU.add))
            nc.vector.tensor_copy(row_i, row).then_inc(sem("row_i"), 1)
            dve.wait_ge(sem("lst_ps"), L + 1)
            nc.vector.tensor_copy(slots[:, :, 0], ps[:, 2, 0:COLS])
            nc.vector.tensor_copy(slots[:, :, 1], ps[:, 2, 128:128 + COLS]).then_inc(sem("slots"), 1)

            def pair(i, b):
                dve.wait_ge(sem(f"x_ps{L}"), i * 2 + (b + 1))
                nc.vector.tensor_copy(xT[:, 4:8, :].rearrange("p k s -> p (k s)"), bank(1)).then_inc(sem(f"xT_d{L}"), 1)
                dve.wait_ge(sem(f"sil{L}"), i * 2 + (b + 1))
                nc.vector.tensor_tensor(act_a, sil, ps[:, 2 + b, FH:2 * FH], ALU.mult).then_inc(sem(f"a{L}"), 1)
                dve.wait_ge(sem(f"y_ps{L}"), i * 2 + (b + 1))
                dve.wait_ge(sem(f"y_free{L}"), i * 2 + (b + 1))
                nc.vector.tensor_copy(y_sb[:, b, 512:1024], bank(6)).then_inc(sem(f"y_d{L}"), 1)

            dve.sem_inc(sem(f"y_d{L}"), 1)
            with dve.Fori(0, PAIRS // 2) as i:
                for b in range(2):
                    pair(i, b)
            dve.wait_ge(sem("cnt"), L + 1)
            most = dve.value_load(cnt_i[0:1, L:L + 1], min_val=0, max_val=T)
            with dve.If(most > WIN):
                with dve.Fori(PAIRS // 2, PASSES * PAIRS // 2) as i:
                    for b in range(2):
                        pair(i, b)
            dve.wait_ge(sem("y12_in"), 64 * L + 64)
            for t, (t0, tn) in enumerate(TOK):
                link(nc.vector.tensor_scalar(y12[0:tn, 0, t, :], y12[0:tn, 0, t, :], gate_w[0:tn, t, 0:1], None, ALU.mult))
                nc.vector.scalar_tensor_tensor(out=y12[0:tn, 0, t, :], in0=y12[0:tn, 1, t, :], scalar=gate_w[0:tn, t, 1:2],
                                               in1=y12[0:tn, 0, t, :], op0=ALU.mult, op1=ALU.add).then_inc(sem("comb"), 1)
            for k in range(KD):
                dve.wait_ge(sem("cT_ps"), 8 * L + k + 1)
                add_h(k, bank(k % 4, T))
            norm(f"ple{L}", h_t, hn_t, G_PLE[L])
            for m in range(KD):
                dve.wait_ge(sem("pg_sig"), 8 * L + m + 1)
                nc.vector.tensor_tensor(sg[:, m % 4, :], sg[:, m % 4, :], prj[:, m, :], ALU.mult).then_inc(sem("pg_in"), 1)
                dve.wait_ge(sem("pg_in"), 8 * L + m + 1)
                nc.vector.tensor_tensor(h_t[:, m, :], h_t[:, m, :], sg[:, m % 4, :], ALU.add).then_inc(sem("h_upd"), 1)

        moe(0)

        norm("mix1", h_t, hn_t, G_MIX[1])
        dve.wait_ge(sem("ws_in"), 48)
        nc.vector.tensor_tensor(wsT, wsT, bc(const[:, C_WM:C_WM + P].unsqueeze(1), [P, 8, P]), ALU.mult).then_inc(sem("ws_m"), 1)
        nc.vector.tensor_tensor(wsS, wsS, bc(const[0:NS_, C_WSM:C_WSM + NS_].unsqueeze(1), [NS_, 8, NS_]), ALU.mult).then_inc(sem("ws_m"), 1)
        dve.wait_ge(sem("rs_ps"), 1)
        nc.vector.tensor_copy(rs[:, :, 0:P], ps[:, 5:7, :].rearrange("p b (g r) -> p (b g) r", g=4)).then_inc(sem("rs"), 1)
        nc.vector.tensor_copy(rs[:, :, P:160], ps[:, 4, 0:256].rearrange("p (g r) -> p g r", g=8)).then_inc(sem("rs"), 1)
        for t in range(FT):
            dve.wait_ge(sem("vt_ps"), t + 1)
            nc.vector.tensor_copy(v_tok[:, 0:2, t * P:(t + 1) * P], ps[:, 4 + t % 2, 0:256].rearrange("p (t f) -> p t f", t=2)).then_inc(sem("v_sb"), 1)
            nc.vector.tensor_copy(v_tok[0:NS_, 2, t * P:(t + 1) * P], ps[0:NS_, 4 + t % 2, 256:384]).then_inc(sem("v_sb"), 1)
        dve.wait_ge(sem("v_sb"), 2 * FT)
        for t, (t0, tn) in enumerate(TOK):
            for c in range(6):
                ins = nc.vector.bn_stats(bst[0:tn, 36 * t + 6 * c:36 * t + 6 * c + 6], v_tok[0:tn, t, 512 * c:512 * c + 512])
            link(ins)
            nc.vector.bn_aggr(mv[0:tn, t, :], bst[0:tn, 36 * t:36 * t + 36]).then_inc(sem("v_mv"), 1)
        nc.vector.memset(vst[:, :, :], 1.0).then_inc(sem("vst_init"), 1)
        dve.wait_ge(sem("v_std"), 2)
        link(nc.vector.reciprocal(vst[:, :, 1], vst[:, :, 0]))
        for t, (t0, tn) in enumerate(TOK):
            nc.vector.tensor_scalar(v_tok[0:tn, t, :], v_tok[0:tn, t, :], mv[0:tn, t, 0:1], vst[0:tn, t, 1:2],
                                    ALU.subtract, ALU.mult).then_inc(sem("v_n"), 1)

        for t in range(FT):
            g = t // 3
            gv, bv = par[:, G_V + t:G_V + t + 1], par[:, B_V + t:B_V + t + 1]
            if t:
                dve.wait_ge(sem("g_sb"), t)
            for c0, cn, r0 in ((0, P, 0), (P, P, 0), (2 * P, NS_, P)):
                ins = nc.vector.scalar_tensor_tensor(out=tm[:, c0:c0 + cn], in0=rs[:, g, r0:r0 + cn], scalar=bv,
                                                     in1=bs[:, g, r0:r0 + cn], op0=ALU.mult, op1=ALU.add)
            link(ins)
            dve.wait_ge(sem("sp_ps"), t + 1)
            link(nc.vector.scalar_tensor_tensor(out=sr, in0=bank(6 + t % 2, T), scalar=gv, in1=tm, op0=ALU.mult, op1=ALU.add))
            dve.wait_ge(sem("z_sb"), FT + t + 1)
            nc.vector.tensor_tensor(uT[:, t, :], uT[:, t, :], sr, ALU.mult).then_inc(sem("g_sb"), 1)
        dve.wait_ge(sem("vs_ps"), 1)
        vps = ps[:, 4:6, :].rearrange("p b n -> p (b n)")[:, 0:FT * NS_].rearrange("p (f t) -> p f t", t=NS_)
        link(nc.vector.tensor_tensor(vsT, vps, bc(par[:, G_V:G_V + FT].unsqueeze(2), [P, FT, NS_]), ALU.mult))
        nc.vector.tensor_tensor(vsT, vsT, bc(par[:, B_V:B_V + FT].unsqueeze(2), [P, FT, NS_]), ALU.add).then_inc(sem("vs"), 1)
        for m in range(KD):
            dve.wait_ge(sem("so_ps"), m + 1)
            add_h(m, bank(m % 4, T))
        moe(1)
        norm("fin", h_t, hn_t, G_FIN)

    @block.tensor
    def _(pe):
        mm = nc.tensor.matmul

        def norm(name, sq):
            n = N_IDX[name]
            if n:
                pe.wait_ge(sem("std"), n)
            for k in range(N_K[name]):
                pe.wait_ge(sem("sq"), N_BASE[name] + k + 1)
                last = mm(bank(7, T), ones, sq[:, k, :], start=(k == 0), stop=(k == N_K[name] - 1))
                if k == 0:
                    free_with(last)
            last.then_inc(sem("ss_ps"), 1)

        pe.sem_inc(sem("kv_free"), 2)
        pe.wait_ge(sem("const_in"), 16)
        norm("mix0", hn_t)
        wait_slots(pe, S_IN, S_IN + 3)
        at = 0
        for m, mn in enumerate([P] * 5 + [RO] * 2):
            for k in range(KD):
                if m == 0:
                    pe.wait_ge(sem("hn"), N_BASE["mix0"] + k + 1)
                last = mm(ps[0:mn, m, 0:T], ring(S_IN, at, mn), hn_t[:, k, :], start=(k == 0), stop=(k == KD - 1))
                at += mn
            last.then_inc(sem("a_ps"), 1)
        owe(3)
        norm("cq", sq_a)
        norm("ckv", sq_c)
        pe.wait_ge(sem("a_sb"), 5)
        pe.wait_ge(sem("hn"), N_BASE["ckv"] + 2)
        for t, (t0, tn) in enumerate(TOK):
            for c in range(2):
                last = nc.tensor.transpose(ps[0:tn, t // 2, (t % 2) * KV + c * P:(t % 2) * KV + c * P + P],
                                           ckvT[:, c, t0:t0 + tn], ident)
        last.then_inc(sem("ckt_ps"), 1)
        wait_slots(pe, S_QB, S_QB + 3)

        def q_tile(j, b):
            for k in range(3):
                last = mm(bank(b, T), ring(S_QB, j * 384 + k * P, P), cq[:, k, :], start=(k == 0), stop=(k == 2))
            return last

        for h in range(H):
            if h >= 2:
                pe.wait_ge(sem("qn_sb"), h - 1)
            q_tile(h, 2 + h % 2).then_inc(sem("qn_ps"), 1)
        pe.wait_ge(sem("kr"), 1)
        pe.wait_ge(sem("std"), N_IDX["ckv"] + 1)
        for p in range(H // 2):
            if p >= 2:
                pe.wait_ge(sem("qr"), p - 1)
            q_tile(H + 2 * p, 4 + 2 * (p % 2))
            q_tile(H + 2 * p + 1, 5 + 2 * (p % 2)).then_inc(sem("qr_ps"), 1)
        owe(3)
        wait_slots(pe, S_UK, S_UK + 1)
        pe.wait_ge(sem("ckt"), 2)
        for h in range(H):
            pe.wait_ge(sem("qn_sb"), h + 1)
            for c in range(2):
                if h >= 2:
                    pe.wait_ge(sem("ql_a" if c == 0 else "ql_d"), h - 1)
                mm(bank((2 * h + c) % 4, T), ring(S_UK, h * KV + c * P, P), qn[:, h, :], start=True, stop=True).then_inc(sem("ql_ps"), 1)
            if h == 0:
                pe.wait_ge(sem("qn_sb"), H)
        owe(1)
        pe.wait_ge(sem("ql_a"), H)
        pe.wait_ge(sem("ql_d"), H)
        pe.wait_ge(sem("qr"), H // 2)

        def scores(h):
            u = h % 2
            if h >= 2:
                pe.wait_ge(sem("masked"), h - 1)
            for c0, q0, kn in ((0, 0, P), (P, P, NP_)):
                free_with(mm(ps[:, u, c0:c0 + kn], ql[:, h, 0, q0:q0 + P], ckvT[:, 0, 0:kn], start=True, stop=False))
                mm(ps[:, u, c0:c0 + kn], ql[:, h, 1, q0:q0 + P], ckvT[:, 1, 0:kn], start=False, stop=False)
                last = mm(ps[:, u, c0:c0 + kn], qr[:, h, q0:q0 + P], krT[:, 0:kn], start=False, stop=True)
            last.then_inc(sem("sc_ps"), 1)

        def turn_p(h):
            pe.wait_ge(sem("p_n"), h + 1)
            for j in range(3):
                last = nc.tensor.transpose(ps[:, 2, j * P:(j + 1) * P], p_p[:, h % 2, j * P:(j + 1) * P], ident)
            last.then_inc(sem("pt_ps"), 1)

        def apply_p(h):
            pe.wait_ge(sem("pt_sb"), h + 1)
            if h >= 1:
                pe.wait_ge(sem("ol"), h)
            for c in range(2):
                mm(ps[:, 3, c * NP_:(c + 1) * NP_], ckt[:, 0, c * P:(c + 1) * P], pt_p[:, 0:NP_], start=True, stop=False)
                last = mm(ps[:, 3, c * NP_ + P:(c + 1) * NP_], ckt[:, 1, c * P:(c + 1) * P], pt_p[:, NP_:384], start=False, stop=True)
            last.then_inc(sem("pv_ps"), 1)

        def q_of(r, b, c):
            return qs[0:RO, 2, 4 * r + b, :] if c == 2 else qs[:, c, 4 * r + b, :]

        def s_chunk(r, cc):
            u = cc % 2
            pe.wait_ge(sem(f"kv_full{u}"), 16 * (48 * r + 16 * (cc // 2) + 16))
            if cc == 0 and r == 0:
                pe.wait_ge(sem("qs"), 3)
            for c in range(3):
                for b in range(4):
                    mov = kv[:, u, b, :, c * P:(c + 1) * P] if c < 2 else kv[0:RO, u, b, :, 256:384]
                    last = mm(ps[32 * b:32 * b + 32, 4 + cc // 2, (cc % 2) * 256:(cc % 2) * 256 + 256],
                              q_of(r, b, c), mov, start=(c == 0), stop=(c == 2))
            last.then_inc(sem("kv_free"), 1)
            if cc == 3:
                for c in range(3):
                    for b in range(4):
                        mov = ckvT[:, c, NP_:T] if c < 2 else krT[:, NP_:T]
                        last = mm(ps[32 * b:32 * b + 32, 6, 0:NS_], q_of(r, b, c), mov, start=(c == 0), stop=(c == 2))
                last.then_inc(sem("s_ps"), 1)

        def s_turn(r):
            pe.wait_ge(sem("s_pn"), r + 1)
            for g in range(8):
                nc.tensor.transpose(ps[:, 4 + g // 4, (g % 4) * P:(g % 4) * P + P], p_s[:, g * P:(g + 1) * P], ident)
            nc.tensor.transpose(ps[0:NS_, 6, 0:P], p_s[:, PAST:PAST + NS_], ident).then_inc(sem("s_pt_ps"), 1)

        def v_chunk(r, cc):
            u = cc % 2
            if cc == 0:
                pe.wait_ge(sem("s_pt_a"), r + 1)
                pe.wait_ge(sem("s_pt_d"), 2 * r + 2)
            pe.wait_ge(sem(f"kv_full{u}"), 16 * (48 * r + 32 + 8 * (cc // 2) + 8))
            for g in range(2):
                for b in range(4):
                    last = mm(ps[32 * b:32 * b + 32, 7, 0:KV], pt_s[:, 2 * cc + g, 32 * b:32 * b + 32],
                              kv[:, u, b, g, 0:KV], start=(cc == 0 and g == 0), stop=False)
            last.then_inc(sem("kv_free"), 1)
            if cc == 3:
                for b in range(4):
                    last = mm(ps[32 * b:32 * b + 32, 7, 0:KV], pt_s[0:NS_, 8, 32 * b:32 * b + 32], ckt[0:NS_, 2, :], start=False, stop=True)
                last.then_inc(sem("s_o_ps"), 1)

        def s_out(r):
            pe.wait_ge(sem("s_ola"), r + 1)
            for c in range(2):
                last = nc.tensor.transpose(ps[:, 6, P + c * P:2 * P + c * P], ola_s[:, c * P:(c + 1) * P], ident)
            last.then_inc(sem("s_ot_ps"), 1)

        scores(0)
        scores(1)
        s_chunk(0, 0), s_chunk(0, 1), turn_p(0), apply_p(0)
        scores(2)
        s_chunk(0, 2), s_chunk(0, 3), turn_p(1), apply_p(1)
        scores(3)
        turn_p(2), apply_p(2)
        scores(4)
        s_turn(0)
        v_chunk(0, 0), v_chunk(0, 1), turn_p(3), apply_p(3)
        scores(5)
        v_chunk(0, 2), v_chunk(0, 3), turn_p(4), apply_p(4)
        s_out(0)
        scores(6)
        s_chunk(1, 0), s_chunk(1, 1), turn_p(5), apply_p(5)
        scores(7)
        s_chunk(1, 2)
        pe.wait_ge(sem("s_ol"), 2)
        s_chunk(1, 3), turn_p(6), apply_p(6)
        turn_p(7), apply_p(7)
        s_turn(1)
        for cc in range(4):
            v_chunk(1, cc)
        s_out(1)
        pe.wait_ge(sem("ol"), H)
        pe.wait_ge(sem("s_ol"), 4)
        wait_slots(pe, S_UV, S_UV + 1)
        for h in range(H):
            if h >= 4:
                pe.wait_ge(sem("o_a" if h % 2 == 0 else "o_d"), (h - 4) // 2 + 1)
            for c in range(2):
                last = mm(bank(h % 4, T), ring(S_UV, c * D + h * P, P), ql[:, h, c, :], start=(c == 0), stop=(c == 1))
            last.then_inc(sem("o_ps"), 1)
        owe(1)
        pe.wait_ge(sem("o_a"), H // 2)
        pe.wait_ge(sem("o_d"), H // 2)
        for m in range(KD):
            if m % 2 == 0:
                wait_slots(pe, S_O + m // 2, S_O + m // 2 + 1)
            if m >= 4:
                pe.wait_ge(sem("h_upd"), m - 3)
            for k in range(H):
                last = mm(bank(WO_BANK[m % 4], T), ring(S_O, m * D + k * P, P), oT[:, k, :], start=(k == 0), stop=(k == H - 1))
                if k == 0:
                    free_with(last)
            last.then_inc(sem("wo_ps"), 1)
            if m % 2 == 1:
                owe(1)

        def moe(L):
            norm(f"ffn{L}", hn_t)
            pe.wait_ge(sem("wr_in"), 32)
            for t, (t0, tn) in enumerate(TOK):
                for k in range(KD):
                    if t == 0:
                        pe.wait_ge(sem("hn"), N_BASE[f"ffn{L}"] + k + 1)
                    last = mm(ps[0:tn, 0, 36 * t:36 * t + 36], hn_t[:, k, t0:t0 + tn], w_r[:, L, k, :], start=(k == 0), stop=(k == KD - 1))
            last.then_inc(sem("lg_ps"), 1)
            for t, (t0, tn) in enumerate(TOK):
                if t == 2:
                    pe.wait_ge(sem("hr_a"), 3 * L + 1)
                    pe.wait_ge(sem("hr_d"), 3 * L + 1)
                for k in range(KD):
                    last = nc.tensor.transpose(ps[0:tn, 2 + 2 * (t % 2) + k // 4, (k % 4) * P:(k % 4) * P + P], hn_t[:, k, t0:t0 + tn], ident)
                last.then_inc(sem("hr_ps"), 1)
            pe.wait_ge(sem("sel"), L + 1)
            lt = const[:, C_LT:C_LT + P]
            for t in range(3):
                for j in range(t):
                    mm(ps[:, 1, 32 * t:32 * t + 32], ones, sel[:, j, :], start=(j == 0), stop=False)
                mm(ps[:, 1, 32 * t:32 * t + 32], lt, sel[:, t, :], start=(t == 0), stop=True)
            for t, (t0, tn) in enumerate(TOK):
                last = mm(ps[:, 1, 96:128], ones[0:tn, :], sel[0:tn, t, :], start=(t == 0), stop=(t == 2))
            last.then_inc(sem("rank_ps"), 1)
            pe.wait_ge(sem("pT_in"), 16 * L + 16)
            pe.wait_ge(sem("hr_a"), 3 * L + 3)
            pe.wait_ge(sem("hr_d"), 3 * L + 3)
            wait_slots(pe, S_PROJ[L], S_PROJ[L] + 1)
            for m in range(KD):
                if m >= 4:
                    pe.wait_ge(sem("prj"), 8 * L + m - 3)
                for k in range(2):
                    last = mm(bank(4 + m % 4, T), ring(S_PROJ[L], m * 256 + k * P, P), pT[:, k, :], start=(k == 0), stop=(k == 1))
                last.then_inc(sem("prj_ps"), 1)
            owe(1)
            pe.wait_ge(sem("list_in"), 16 * L + 16)
            li = lst.rearrange("c (r v) -> c v r", v=2)
            for v in range(2):
                last = nc.tensor.transpose(ps[:, 2, P * v:P * v + COLS], li[:, v, :], ident[0:COLS, 0:COLS])
                if v == 0:
                    free_with(last)
            last.then_inc(sem("lst_ps"), 1)
            pe.wait_ge(sem("slots"), L + 1)
            pe.wait_ge(sem("prj"), 8 * L + KD)

            def pair(i, b, tail):
                n1 = i * 2 + (b + 1)
                pe.wait_ge(sem(f"x_got{L}_{b}"), i * 16 + 16)
                for k in range(KD):
                    last = nc.tensor.transpose(ps[:, k // 4, (k % 4) * P:(k % 4) * P + P], x_sel[:, b, k * P:(k + 1) * P], ident)
                last.then_inc(sem(f"x_ps{L}"), 1)
                pe.wait_ge(sem(f"xT_a{L}"), n1)
                pe.wait_ge(sem(f"xT_d{L}"), n1)
                s0 = S_MOE[L] + 6 * b
                if tail is None:
                    for j in range(4):
                        pe.wait_ge(sem(f"slot_full{(s0 + j) % RING}"), i * 16 + 16 * ((s0 + j) // RING + 1))
                    gu = [ring(s0 + 2 * a, 0, 2 * SLOT) for a in range(2)]
                    dn = [ring(s0 + 4 + a, 0, SLOT) for a in range(2)]
                else:
                    pe.wait_ge(sem(f"tail_w{L}"), tail * 128 + 64 * (b + 1))
                    gu = [tail_gu[:, a].rearrange("p s n -> p (s n)") for a in range(2)]
                    dn = tail_dn
                for k in range(KD):
                    for a in range(2):
                        last = mm(ps[64 * a:64 * a + 64, 2 + b, :], xT[:, k, 64 * a:64 * a + 64], gu[a][:, k * 512:(k + 1) * 512],
                                  start=(k == 0), stop=(k == KD - 1))
                last.then_inc(sem(f"h_ps{L}"), 1)
                pe.wait_ge(sem(f"a{L}"), n1)
                for k in range(2):
                    last = nc.tensor.transpose(ps[:, 4, k * P:(k + 1) * P], act_a[:, k * P:(k + 1) * P], ident)
                    if k == 0 and tail is None:
                        last.then_inc(sem("slot_free"), 4)
                last.then_inc(sem(f"aT_ps{L}"), 1)
                pe.wait_ge(sem(f"aT{L}"), n1)
                pe.wait_ge(sem(f"y_a{L}"), n1)
                pe.wait_ge(sem(f"y_d{L}"), n1)
                if tail is None:
                    for j in (4, 5):
                        pe.wait_ge(sem(f"slot_full{(s0 + j) % RING}"), i * 16 + 16 * ((s0 + j) // RING + 1))
                for k in range(2):
                    for n in range(2):
                        for a in range(2):
                            last = mm(ps[64 * a:64 * a + 64, 5 + n, :], aT[:, k, 64 * a:64 * a + 64],
                                      dn[a][:, k * D + n * 512:k * D + n * 512 + 512], start=(k == 0), stop=(k == 1))
                last.then_inc(sem(f"y_ps{L}"), 1)
                if tail is None:
                    pe.drain().then_inc(sem("slot_free"), 2)

            with pe.Fori(0, PAIRS // 2) as i:
                for b in range(2):
                    pair(i, b, None)
            pe.wait_ge(sem("cnt"), L + 1)
            most = pe.value_load(cnt_i[0:1, L:L + 1], min_val=0, max_val=T)
            with pe.If(most > WIN):
                with pe.Fori(0, (PASSES - 1) * PAIRS // 2) as j:
                    for b in range(2):
                        pair(j + PAIRS // 2, b, j)
            pe.wait_ge(sem("comb"), 3 * L + 3)
            for k in range(KD):
                if k >= 4:
                    pe.wait_ge(sem("h_upd"), 8 * (1 if L == 0 else 4) + k - 3)
                for t, (t0, tn) in enumerate(TOK):
                    last = nc.tensor.transpose(ps[:, k % 4, t0:t0 + tn], y12[0:tn, 0, t, k * P:(k + 1) * P], ident[0:tn, 0:tn])
                last.then_inc(sem("cT_ps"), 1)
            norm(f"ple{L}", hn_t)
            for m in range(KD):
                s = S_GATE[L] + m // 2
                if m % 2 == 0:
                    wait_slots(pe, s, s + 1)
                if m >= 4:
                    pe.wait_ge(sem("pg_sig"), 8 * L + m - 3)
                for k in range(KD):
                    if m == 0:
                        pe.wait_ge(sem("hn"), N_BASE[f"ple{L}"] + k + 1)
                    last = mm(bank(m % 4, T), ring(s, (m % 2) * D + k * P, P), hn_t[:, k, :], start=(k == 0), stop=(k == KD - 1))
                    if k == 0:
                        free_with(last)
                last.then_inc(sem("pg_ps"), 1)
                if m % 2 == 1:
                    owe(1)

        moe(0)

        norm("mix1", hn_t)
        pe.wait_ge(sem("ws_m"), 2)
        for g in range(8):
            mm(ps[:, 5 + g // 4, (g % 4) * P:(g % 4) * P + P], ones, wsT[:, g, :], start=True, stop=True)
        for g in range(8):
            last = mm(ps[:, 4, 32 * g:32 * g + 32], ones[0:NS_, :], wsS[:, g, :], start=True, stop=True)
        last.then_inc(sem("rs_ps"), 1)

        def z_tile(i):
            s = S_SGU + i // 2
            if i % 2 == 0:
                wait_slots(pe, s, s + 1)
            if i >= 4:
                pe.wait_ge(sem("z_sb"), i - 3)
            for k in range(KD):
                if i == 0:
                    pe.wait_ge(sem("hn"), N_BASE["mix1"] + k + 1)
                last = mm(bank(i % 4, T), ring(s, (i % 2) * D + k * P, P), hn_t[:, k, :], start=(k == 0), stop=(k == KD - 1))
                if k == 0:
                    free_with(last)
            last.then_inc(sem("z_ps"), 1)
            if i % 2 == 1:
                owe(1)

        def v_turn(t):
            pe.wait_ge(sem("z_sb"), t + 1)
            if t < 2:
                pe.wait_ge(sem("rs"), 2)
            else:
                pe.wait_ge(sem("v_sb"), 2 * (t - 1))
            for j, (t0, tn) in enumerate(TOK):
                last = nc.tensor.transpose(ps[0:tn, 4 + t % 2, j * P:j * P + P], vT[:, t % 2, t0:t0 + tn], ident)
            last.then_inc(sem("vt_ps"), 1)

        def mix(t):
            if t == 0:
                pe.wait_ge(sem("v_n"), 3)
            if t >= 2:
                pe.wait_ge(sem("g_sb"), t - 1)
            fs = slice(t * P, (t + 1) * P)
            for j in range(2):
                mm(ps[:, 6 + t % 2, j * P:(j + 1) * P], v_tok[:, j, fs], wsT[:, t // 3, :], start=True, stop=True)
            mm(ps[:, 6 + t % 2, NP_:T], v_tok[0:NS_, 2, fs], wsS[:, t // 3, :], start=True, stop=True).then_inc(sem("sp_ps"), 1)

        for t in range(FT):
            z_tile(t)
            if t >= 1:
                v_turn(t - 1)
        LAG = 7
        for t in range(FT):
            z_tile(FT + t)
            if t == 0:
                v_turn(FT - 1)
            if t >= LAG:
                mix(t - LAG)
        for t in range(FT - LAG, FT):
            mix(t)
        pe.wait_ge(sem("v_sb"), 2 * FT)
        for t in range(FT):
            last = nc.tensor.transpose(ps[:, 4 + t // 16, (t % 16) * NS_:(t % 16) * NS_ + NS_], v_tok[0:NS_, 2, t * P:(t + 1) * P], ident[0:NS_, 0:NS_])
        last.then_inc(sem("vs_ps"), 1)
        pe.wait_ge(sem("z_sb"), 2 * FT)
        for m in range(KD):
            for k in range(FT):
                at = m * FT + k
                s = S_OUT + at // 16
                if at % 16 == 0:
                    wait_slots(pe, s, s + 1)
                if m == 0:
                    pe.wait_ge(sem("g_sb"), k + 1)
                if k == 0 and m >= 4:
                    pe.wait_ge(sem("h_upd"), 24 + m - 3)
                last = mm(bank(m % 4, T), ring(s, (at % 16) * P, P), uT[:, k, :], start=(k == 0), stop=(k == FT - 1))
                if k == 0:
                    free_with(last)
                if at % 16 == 15 and k != FT - 1:
                    last.then_inc(sem("slot_free"), 1)
            last.then_inc(sem("so_ps"), 1)
            if (m * FT + FT) % 16 == 0:
                owe(1)
        moe(1)
        norm("fin", hn_t)


def _tiles(w, cols):
    k = w.shape[0] // P
    return np.concatenate([w[:, c].reshape(k, P, -1).transpose(1, 0, 2).reshape(P, -1) for c in cols], 1)


def _slots(a):
    return a.reshape(P, -1, SLOT).transpose(1, 0, 2)


def _stream(i):
    cols = lambda n: [slice(c, c + P) for c in range(0, n, P)]
    swap = lambda c0: [*range(c0 + 32, c0 + 64), *range(c0, c0 + 32)]
    w_in, w_qb = i["mla_w_in"][0], i["mla_w_qb"][0]
    a = QL + KV
    parts = [_slots(_tiles(w_in, cols(a) + [slice(a, a + RO), swap(a)]))]
    q = [slice(192 * h, 192 * h + 128) for h in range(H)]
    for p in range(H // 2):
        r = [192 * (2 * p + j) + 128 for j in range(2)]
        q += [[*range(r[0], r[0] + RO), *range(r[1], r[1] + RO)], swap(r[0]) + swap(r[1])]
    parts.append(_slots(_tiles(w_qb, q)))
    parts.append(_slots(i["mla_w_uk"][0].transpose(2, 1, 0).reshape(P, -1)))
    parts.append(_slots(i["mla_w_uv"][0].reshape(2, P, -1).transpose(1, 0, 2).reshape(P, -1)))
    parts.append(_slots(_tiles(i["mla_w_o"][0], cols(D))))
    for L in range(2):
        parts.append(_slots(_tiles(i["ple_w_proj"][L], cols(D))))
        gu = np.concatenate([i["moe_w_gate"][L], i["moe_w_up"][L]], 2).reshape(NE, KD, P, 2 * FH)
        gu = gu.transpose(0, 2, 1, 3).reshape(PAIRS, 2, P, 2, SLOT).transpose(0, 1, 3, 2, 4).reshape(PAIRS, 4, P, SLOT)
        dn = i["moe_w_down"][L].reshape(PAIRS, 2, 2, P, D).transpose(0, 1, 3, 2, 4).reshape(PAIRS, 2, P, SLOT)
        parts.append(np.concatenate([gu, dn], 1).reshape(PAIRS * 6, P, SLOT))
        parts.append(_slots(_tiles(i["ple_w_gate"][L], cols(D))))
        if L == 0:
            w = i["sgu_w_in"][0]
            parts.append(_slots(_tiles(w, [slice(FF + c, FF + c + P) for c in range(0, FF, P)] + cols(FF))))
            parts.append(_slots(_tiles(i["sgu_w_out"][0], cols(D))))
    return np.concatenate(parts, 0)


def _constants():
    c, ac = np.zeros((P, N_CONST), np.float32), np.zeros((P, N_ACONST), np.float32)
    r, q = np.arange(P)[:, None], np.arange(P)[None, :]
    c[:, C_ID:C_ID + P] = np.eye(P)
    c[:, C_ONE:C_ONE + P] = 1
    for at in (0, 2 * P):
        ac[:, C_MSK + at:C_MSK + at + P] = np.where(q <= r, 0, NEG)
    rb, rs_, key = r // 32, r % DEC_S, np.arange(NS_)[None, :]
    for rnd in range(2):
        ok = (key // DEC_S == 4 * rnd + rb) & (key % DEC_S <= rs_)
        ac[:, C_SMSK + NS_ * rnd:C_SMSK + NS_ * (rnd + 1)] = np.where(ok, 0, NEG)
    c[:, C_LT:C_LT + P] = r < q
    c[:, C_WM:C_WM + P] = r <= q
    c[0:NS_, C_WSM:C_WSM + NS_] = ((r // DEC_S == q // DEC_S) & (r % DEC_S <= q % DEC_S))[0:NS_, 0:NS_]
    pos = np.concatenate([np.arange(NP_), np.tile(PAST + np.arange(DEC_S), DEC_B)]).astype(np.float32)
    inv = (1.0 / (np.float32(10000.0) ** (np.arange(0, RO, 2, dtype=np.float32) / np.float32(RO)))).astype(np.float32)
    ang = (pos[None, :] * inv[np.arange(P) % 32][:, None]).astype(np.float32)
    ac[:, C_COS:C_COS + T] = np.cos(ang)
    ac[:, C_SIN:C_SIN + T] = np.sin(ang) * np.where(np.arange(P) % 64 < 32, -1, 1)[:, None]
    c[:, C_IOTA:C_IOTA + EPG] = np.arange(EPG)
    c[NS_:, C_INV + 2] = 1e6
    for t in range(3):
        for k in range(2):
            c[:, C_TV + 4 * t + 2 * k] = P * t + np.arange(P)
            c[:, C_TV + 4 * t + 2 * k + 1] = k * T + P * t + np.arange(P)
    return c, ac


def _params(i):
    col = lambda v: v.reshape(-1, P).T
    return np.concatenate([col(v) for v in (
        i["g_mix"][0], i["g_mix"][1], i["g_ffn"][0], i["g_ffn"][1], i["g_ple"][0], i["g_ple"][1], i["g_final"],
        i["mla_g_q"][0], i["mla_g_kv"][0], i["sgu_b_in"][0], i["sgu_g_v"][0], i["sgu_b_v"][0])], 1)


def kernel(**inputs):
    import concourse.bacc as bacc
    from concourse.bass_utils import run_bass_kernel_spmd

    i = {k: np.asarray(v) for k, v in inputs.items()}
    feat = lambda a: a.T.reshape(-1, P, a.shape[0]).transpose(1, 0, 2)
    tok = lambda p, s: np.concatenate([p.reshape(NP_, -1), s.reshape(NS_, -1)], 0)
    ckv, kr = i["cache_ckv"][0], i["cache_krope"][0]
    n_phys = ckv.shape[0]
    w_s, b_s = i["sgu_w_s"][0], i["sgu_b_s"][0]
    w_r = np.concatenate([i["moe_w_rg"], i["moe_w_re"]], 2)
    b_r = np.concatenate([i["moe_b_rg"], i["moe_b_re"]], 1)
    arrays = {
        "stream": _stream(i),
        "x": feat(tok(i["x_prompt"], i["x_sample"])),
        "p": np.stack([feat(tok(i["p_prompt"][L], i["p_sample"][L])) for L in range(2)], 1),
        "ckv_t": ckv.transpose(0, 2, 1).reshape(n_phys, 2, P, PAGE).transpose(0, 2, 1, 3).reshape(n_phys, P, 256),
        "kr_t": kr.transpose(0, 2, 1),
        "ckv_n": ckv,
        "ptab": i["page_table"].reshape(1, -1).astype(np.int32),
        "par": _params(i),
        "const": _constants()[0],
        "aconst": _constants()[1],
        "w_r": w_r.reshape(2, KD, P, G + NE).transpose(2, 0, 1, 3),
        "b_r": np.broadcast_to(b_r, (P, 2, G + NE)),
        "ws": w_s.transpose(2, 0, 1),
        "wss": np.tile(w_s[:, :DEC_S, :DEC_S].transpose(2, 0, 1), (DEC_B, 1, DEC_B)),
        "bs": np.broadcast_to(np.concatenate([b_s, np.tile(b_s[:, :DEC_S], (1, DEC_B))], 1), (P, 8, 160)),
    }
    arrays = {k: np.ascontiguousarray(v) for k, v in arrays.items()}
    nc = bacc.Bacc("TRN2", target_bir_lowering=False, num_devices=1)
    io = {k: nc.dram_tensor(k, v.shape, mybir.dt.from_np(v.dtype), kind="ExternalInput").ap() for k, v in arrays.items()}
    outs = {"y_out": (P, KD, T), "ckv_out": (P, 2, T), "kr_out": (RO, T), "vs_out": (P, FT, NS_)}
    for k, shape in outs.items():
        io[k] = nc.dram_tensor(k, shape, FP, kind="ExternalOutput").ap()
    io["lists"] = [nc.dram_tensor(f"list{L}", (COLS * P, 2), FP).ap() for L in range(2)]
    io["hn_rows"] = [nc.dram_tensor(f"hn_rows{L}", (T, D), FP).ap() for L in range(2)]
    io["y_rows"] = [nc.dram_tensor(f"y_rows{L}", (2 * T, D), FP).ap() for L in range(2)]
    io["n_phys"] = n_phys
    build(nc, io)
    got = run_bass_kernel_spmd(nc, [arrays], core_ids=[0]).results[0]
    rows = lambda a: a.transpose(2, 1, 0).reshape(a.shape[2], -1)
    y, c, v = rows(got["y_out"]), rows(got["ckv_out"]), rows(got["vs_out"])
    r = got["kr_out"].T
    new = (1, DEC_B, DEC_S, -1)
    return (y[:NP_].reshape(1, NP_, D), y[NP_:].reshape(DEC_B, DEC_S, D),
            c[:NP_].reshape(1, 1, NP_, KV), r[:NP_].reshape(1, 1, NP_, RO),
            c[NP_:].reshape(new), r[NP_:].reshape(new), v.reshape(new))
```

```python
from contextlib import ExitStack

import numpy as np

import concourse.bass as bass
from concourse import mybir

FP = mybir.dt.float32
I32 = mybir.dt.int32
ACT = mybir.ActivationFunctionType
ALU = mybir.AluOpType
AX = mybir.AxisListType

P = 128
D, KD = 1024, 8
NP_, NS_ = 256, 32
T = NP_ + NS_
TOK = [(0, 128), (128, 128), (256, 32)]
H, DEC_B, DEC_S = 8, 8, 4
QL, KV, RO = 384, 256, 64
PAST, PAGE = 1024, 128
PAGES = PAST // PAGE
SCALE = (128 + 64) ** -0.5
FF, FT = 3072, 24
G, EPG, NE, FH = 4, 8, 32, 256
WIN = 64
PAIRS = NE // 2
PASSES = -(-T // WIN)
COLS = PASSES * PAIRS + 2
OOB = 9999.0
NEG = -1e30

SLOT, RING = 2048, 12
S_IN, S_QB, S_UK, S_UV, S_O = 0, 3, 6, 7, 8
S_PROJ = [12, 149]
S_MOE = [13, 150]
S_GATE = [109, 246]
S_SGU, S_OUT = 113, 137
N_SLOTS = 250

C_ID, C_ONE, C_LT, C_WM, C_WSM, C_IOTA, C_INV, C_TV = 0, 128, 256, 384, 512, 544, 552, 555
N_CONST = 567
C_MSK, C_SMSK, C_COS, C_SIN = 0, 384, 448, 736
N_ACONST = 1024
G_MIX, G_FFN, G_PLE, G_FIN, G_Q, G_KV = [0, 8], [16, 24], [32, 40], 48, 56, 59
B_IN, G_V, B_V = 61, 109, 133
N_PAR = 157

NORMS = [("mix0", 8), ("cq", 3), ("ckv", 2), ("ffn0", 8), ("ple0", 8), ("mix1", 8), ("ffn1", 8),
         ("ple1", 8), ("fin", 8)]
WO_BANK = (4, 5, 6, 0)
N_IDX = {name: n for n, (name, _) in enumerate(NORMS)}
N_BASE = {name: sum(k for _, k in NORMS[:n]) for n, (name, _) in enumerate(NORMS)}
N_K = dict(NORMS)
NEXT = ["mix1", "fin"]
H_STAGE = {"mix0": 0, "ffn0": 1, "ple0": 2, "mix1": 3, "ffn1": 4, "ple1": 5, "fin": 6}


def slot_pos(s):
    return s % RING, s // RING + 1


def build(nc, io):
    with ExitStack() as ctx:
        program(nc, io, ctx)


def program(nc, io, ctx):
    made = {}

    def sem(name):
        if name not in made:
            made[name] = ctx.enter_context(nc.semaphore(name))
        return made[name]

    def sb(name, shape, dt=FP):
        return ctx.enter_context(nc.sbuf_tensor(name + "_sb", shape, dt))

    ring_t = sb("ring", [P, RING * SLOT])
    h_t = sb("h", [P, KD, T])
    hn_t = sb("hn", [P, KD, T])
    const = sb("const", [P, N_CONST])
    par = sb("par", [P, N_PAR])
    w_r = sb("w_r", [P, 2, KD, G + NE])
    b_r = sb("b_r", [P, 2, G + NE])
    eps = sb("eps", [P, 3])
    std_t = sb("std", [P, T])
    rstd_t = sb("rstd", [P, T])
    ptab = sb("ptab", [1, DEC_B * PAGES], I32)
    cnt_i = sb("cnt_i", [P, 2], I32)
    SCR = 21400
    scr = sb("scr", [P, SCR])
    ps = ctx.enter_context(nc.psum_tensor("ps", [P, 8, 512], FP))

    ident, ones = const[:, C_ID:C_ID + P], const[:, C_ONE:C_ONE + P]

    class Area:

        def __init__(self):
            self.at = 0

        def take(self, n, parts=P):
            a = scr[0:parts, self.at:self.at + n]
            self.at += n
            assert self.at <= SCR, self.at
            return a

    A = Area()
    aconst = A.take(N_ACONST)
    cq = A.take(3 * T).rearrange("p (k t) -> p k t", k=3)
    ckvT = A.take(2 * T).rearrange("p (k t) -> p k t", k=2)
    krT = A.take(T, RO)
    ckt = A.take(3 * KV).rearrange("p (t c) -> p t c", t=3)
    qn = A.take(H * T).rearrange("p (h t) -> p h t", h=H)
    ql = A.take(H * 2 * T).rearrange("p (h c t) -> p h c t", h=H, c=2)
    s_p = A.take(2 * 384).rearrange("p (b n) -> p b n", b=2)
    p_p = A.take(2 * 384).rearrange("p (b n) -> p b n", b=2)
    pt_p = A.take(384)
    p_s = A.take(PAST + NS_)
    pt_s = A.take(9 * P).rearrange("p (g r) -> p g r", g=9)
    ola_s = A.take(KV)
    snew = A.take(NS_)
    keys = A.take(2 * 4 * 2 * 384).rearrange("p (u b g n) -> p u b g n", u=2, b=4, g=2)
    rt = pt_s.rearrange("p g r -> p (g r)")[:, 0:2 * T].rearrange("p (a t) -> p a t", a=2)
    sm = A.take(32)
    qr = hn_t[0:RO, :, :]
    sq_a, sq_c = qn[:, 0:3, :], qn[:, 3:5, :]
    oT = qn
    qs = qn.rearrange("p h t -> p (h t)")[:, 0:3 * DEC_B * 32].rearrange("p (c b n) -> p c b n", c=3, b=DEC_B)
    mx, s_mx, s_nmx, s_l = sm[:, 0:2], sm[:, 2:4], sm[:, 4:5], sm[:, 5:7]
    nmx = sm[:, 8:12].rearrange("p (u n) -> p u n", u=2)
    lsum = sm[:, 12:16].rearrange("p (u n) -> p u n", u=2)
    rl = sm[:, 16:20].rearrange("p (u n) -> p u n", u=2)
    fill = p_s[0:COLS, 0:2 * P]

    M = Area()
    pT = M.take(2 * T).rearrange("p (k t) -> p k t", k=2)
    prj = M.take(KD * T).rearrange("p (k t) -> p k t", k=KD)
    x_sel = M.take(2 * D).rearrange("p (b n) -> p b n", b=2)
    xT = M.take(D).rearrange("p (k s) -> p k s", k=KD)
    sil = M.take(FH)
    act_a = M.take(FH)
    aT = M.take(2 * P).rearrange("p (k s) -> p k s", k=2)
    y_sb = M.take(2 * D).rearrange("p (b n) -> p b n", b=2)
    sg = M.take(4 * T).rearrange("p (b t) -> p b t", b=4)
    slots = M.take(2 * COLS).rearrange("p (c v) -> p c v", v=2).bitcast(I32)
    stage = M.take(4).rearrange("p (b v) -> p b v", b=2).bitcast(I32)
    gate_w = M.take(6).rearrange("p (t k) -> p t k", t=3)
    big0 = M.at
    big = M.take(5 * SLOT)
    hn_tok = big[:, 0:3 * D].rearrange("p (t n) -> p t n", t=3)
    tail_gu = big[:, 0:4 * SLOT].rearrange("p (a s n) -> p a s n", a=2, s=2)
    tail_dn = [big[:, 4 * SLOT:5 * SLOT], hn_t[:, :, :].rearrange("p k t -> p (k t)")[:, 0:SLOT]]
    y12 = big[:, 0:6 * D].rearrange("p (k t n) -> p k t n", k=2, t=3)
    R = Area()
    R.at = big0 + 3 * D
    lgt = R.take(3 * 36).rearrange("p (t n) -> p t n", t=3)
    lg, le = lgt[:, :, 0:G], lgt[:, :, G:G + NE].rearrange("p t (g j) -> p t g j", g=G)
    t4 = R.take(3 * G).rearrange("p (t g) -> p t g", t=3)
    t8 = R.take(3 * EPG).rearrange("p (t g) -> p t g", t=3)
    t32 = R.take(3 * NE).rearrange("p (t g j) -> p t g j", t=3, g=G)
    og = R.take(3 * G).rearrange("p (t g) -> p t g", t=3)
    leg = R.take(3 * EPG).rearrange("p (t j) -> p t j", t=3)
    leg2 = R.take(3 * EPG).rearrange("p (t j) -> p t j", t=3)
    oh = R.take(2 * 3 * EPG).rearrange("p (k t j) -> p k t j", k=2, t=3)
    ek = R.take(2 * 3 * NE).rearrange("p (k t e) -> p k t e", k=2, t=3)
    sel = R.take(3 * NE).rearrange("p (t e) -> p t e", t=3)
    gmx = R.take(3)
    gid = R.take(3)
    mk = R.take(6).rearrange("p (k t) -> p k t", k=2)
    ik = R.take(6).rearrange("p (k t) -> p k t", k=2)
    rk = R.take(6).rearrange("p (k t) -> p k t", k=2)
    win = R.take(6).rearrange("p (k t) -> p k t", k=2)
    row = R.take(6).rearrange("p (k t) -> p k t", k=2)
    row_i = R.take(6).rearrange("p (k t) -> p k t", k=2).bitcast(I32)
    dx = R.take(15)
    ex = R.take(15)
    gs = R.take(3)
    den = R.take(3)
    cmx = R.take(1)
    lst = R.take(2 * P, COLS)

    U = Area()
    uT = U.take(FT * T).rearrange("p (f t) -> p f t", f=FT)
    v_tok = U.take(3 * FF).rearrange("p (t f) -> p t f", t=3)
    vT = U.take(2 * T).rearrange("p (b t) -> p b t", b=2)
    wsT = U.take(G * 2 * P).rearrange("p (g r) -> p g r", g=8)
    wsS = U.take(8 * NS_, NS_).rearrange("p (g r) -> p g r", g=8)
    rs = U.take(8 * 160).rearrange("p (g r) -> p g r", g=8)
    bs = U.take(8 * 160).rearrange("p (g r) -> p g r", g=8)
    tm = U.take(T)
    sr = U.take(T)
    bst = U.take(3 * 36)
    mv = U.take(6).rearrange("p (t v) -> p t v", t=3)
    vst = U.take(6).rearrange("p (t v) -> p t v", t=3)
    vsT = hn_t[:, :, :].rearrange("p k t -> p (k t)")[:, 0:FT * NS_].rearrange("p (f t) -> p f t", f=FT)

    lists, hn_rows, y_rows = io["lists"], io["hn_rows"], io["y_rows"]

    def bank(b, n=512):
        return ps[:, b, 0:n]

    def ring(s, at, n):
        o = (s % RING) * SLOT + at
        assert o + n <= RING * SLOT
        return ring_t[:, o:o + n]

    owed = [0]

    def owe(n):
        owed[0] += n

    def free_with(ins):
        if owed[0]:
            ins.then_inc(sem("slot_free"), owed[0])
            owed[0] = 0
        return ins

    def wait_slots(pe, s0, s1):
        for s in range(s0, s1):
            pos, n = slot_pos(s)
            pe.wait_ge(sem(f"slot_full{pos}"), 16 * n)

    block = ctx.enter_context(nc.Block())

    @block.sync
    def _(sp):
        stream = io["stream"]

        def load_slot(s):
            pos, _ = slot_pos(s)
            if s >= RING:
                sp.wait_ge(sem("slot_free"), s - RING + 1)
            sp.dma_start(ring(pos, 0, SLOT), stream[s]).then_inc(sem(f"slot_full{pos}"), 16)

        def load_keys(rnd, cc, u):
            sp.wait_ge(sem("key_free"), cc * 2 + (4 * rnd + u + 1))
            for b in range(4):
                for pg in range(2):
                    at = (4 * rnd + b) * PAGES + 2 * u + pg
                    page = sp.value_load(ptab[0:1, bass.ds(cc * 4 + at, 1)], min_val=0,
                                         max_val=io["n_phys"] - 1)
                    sp.dma_start(keys[:, u, b, pg, :],
                                 io["key_pages"][bass.ds(page, 1)].rearrange("a p n -> (a p) n")
                                 ).then_inc(sem(f"key_full{u}"), 16)

        sp.dma_start(h_t[:, :, :], io["x"]).then_inc(sem("x_in"), 16)
        for s in range(RING):
            load_slot(s)
        sp.wait_ge(sem("ptab_in"), 16)
        for rnd in range(2):
            with sp.Fori(0, 2) as cc:
                for u in range(2):
                    load_keys(rnd, cc, u)
        sp.wait_ge(sem("rows_free"), 8)
        for s in range(RING, 2 * RING):
            load_slot(s)
        def load_rounds(r0, r1):
            with sp.Fori(r0, r1) as i:
                for j in range(RING):
                    sp.wait_ge(sem("slot_free"), i * RING + (j + 1 - RING))
                    sp.dma_start(ring(j, 0, SLOT), stream[bass.ds(i * RING + j, 1)].rearrange("a p n -> (a p) n")
                                 ).then_inc(sem(f"slot_full{j}"), 16)

        load_rounds(2, S_SGU // RING)
        for s in range(S_SGU // RING * RING, S_SGU // RING * RING + RING):
            if s == S_GATE[0] + 2:
                sp.wait_ge(sem("y12_in2"), 32)
            load_slot(s)
        load_rounds(S_SGU // RING + 1, S_GATE[1] // RING)
        for s in range(S_GATE[1] // RING * RING, N_SLOTS):
            if s == S_GATE[1] + 2:
                sp.wait_ge(sem("y12_in2"), 64)
            load_slot(s)

    @block.gpsimd
    def _(pool):
        def moe(L):
            pool.wait_ge(sem("h_upd"), 8 * (1 if L == 0 else 4))
            pool.memset(x_sel, 0.0).then_inc(sem("x_clear"), 1)
            pool.wait_ge(sem("list_clear"), 32)
            pool.wait_ge(sem("row_i"), L + 1)
            for k in range(2):
                for t in range(3):
                    pool.indirect_dma_start(
                        out=lists[L], out_offset=bass.IndirectOffsetOnAxis(ap=row_i[:, k, t:t + 1], axis=0),
                        in_=const[:, C_TV + 4 * t + 2 * k:C_TV + 4 * t + 2 * k + 2], in_offset=None,
                        bounds_check=COLS * P - 1, oob_is_err=False).then_inc(sem("list_put"), 16)
            pool.wait_ge(sem("list_put"), 96 * L + 6 * 16)
            pool.dma_start(lst[:, :], lists[L].rearrange("(c r) v -> c (r v)", r=P)).then_inc(sem("list_in"), 16)
            pool.wait_ge(sem("slots"), L + 1)
            pool.wait_ge(sem("hn_rows"), 48 * L + 3 * 16)
            pool.wait_ge(sem("x_clear"), L + 1)

            def gather(col, b, n_staged):
                pool.tensor_copy(stage[:, b, 0:1], col[:, 0:1]).then_inc(sem(f"staged{L}"), 1)
                pool.wait_ge(sem(f"staged{L}"), n_staged)
                pool.sem_inc(sem("pool_step"), 1)
                pool.indirect_dma_start(
                    out=x_sel[:, b, :], out_offset=None, in_=hn_rows[L],
                    in_offset=bass.IndirectOffsetOnAxis(ap=stage[:, b, 0:1], axis=0),
                    bounds_check=T - 1, oob_is_err=False).then_inc(sem(f"x_got{L}_{b}"), 16)

            def pair(i, b, tail=None, first=False):
                if tail is not None:
                    pool.wait_ge(sem(f"y_ps{L}"), i * 2 + b)
                    w0 = S_MOE[L] + 6 * b
                    for a in range(2):
                        pool.dma_start(tail_gu[:, a, :, :], io["stream"][bass.ds(tail * 12 + (w0 + 2 * a), 2)]
                                       .rearrange("s p n -> p s n")).then_inc(sem(f"tail_w{L}"), 16)
                        pool.dma_start(tail_dn[a], io["stream"][bass.ds(tail * 12 + (w0 + 4 + a), 1)]
                                       .rearrange("s p n -> (s p) n")).then_inc(sem(f"tail_w{L}"), 16)
                pool.wait_ge(sem(f"x_ps{L}"), i * 2 + (b + 1))
                gather(slots[:, bass.ds(i * 2 + (b + 2), 1), :].rearrange("p c v -> p (c v)"), b,
                       i * 4 + (2 * b + 3))
                if not first:
                    pool.wait_ge(sem(f"y_put{L}_{b}"), i * 16)
                pool.sem_inc(sem(f"y_free{L}"), 1)
                pool.tensor_copy(stage[:, b, 1:2], slots[:, bass.ds(i * 2 + b, 1), :].rearrange("p c v -> p (c v)")[:, 1:2]
                                 ).then_inc(sem(f"staged{L}"), 1)
                pool.wait_ge(sem(f"staged{L}"), i * 4 + (2 * b + 4))
                pool.wait_ge(sem(f"y_a{L}"), i * 2 + (b + 2))
                pool.wait_ge(sem(f"y_d{L}"), i * 2 + (b + 2))
                pool.sem_inc(sem("pool_step"), 1)
                pool.indirect_dma_start(
                    out=y_rows[L], out_offset=bass.IndirectOffsetOnAxis(ap=stage[:, b, 1:2], axis=0),
                    in_=y_sb[:, b, :], in_offset=None,
                    bounds_check=2 * T - 1, oob_is_err=False).then_inc(sem(f"y_put{L}_{b}"), 16)

            for b in range(2):
                gather(slots[:, b, :], b, b + 1)
            for b in range(2):
                pair(0, b, first=True)
            with pool.Fori(1, PAIRS // 2) as i:
                for b in range(2):
                    pair(i, b)
            pool.wait_ge(sem("cnt"), L + 1)
            most = pool.value_load(cnt_i[0:1, L:L + 1], min_val=0, max_val=T)
            with pool.If(most > WIN):
                with pool.Fori(0, PASSES - 1) as p:
                    with pool.Fori(0, PAIRS // 2) as q:
                        for b in range(2):
                            pair(p * (PAIRS // 2) + q + PAIRS // 2, b, q)
                for b in range(2):
                    pool.wait_ge(sem(f"x_got{L}_{b}"), 16 * (PASSES * PAIRS // 2 + 1))
                    pool.wait_ge(sem(f"y_put{L}_{b}"), 16 * (PASSES * PAIRS // 2))
            for b in range(2):
                pool.wait_ge(sem(f"x_got{L}_{b}"), 16 * (PAIRS // 2 + 1))
                pool.wait_ge(sem(f"y_put{L}_{b}"), 16 * (PAIRS // 2))
            for t, (t0, tn) in enumerate(TOK):
                for k in range(2):
                    pool.dma_start(y12[0:tn, k, t, :], y_rows[L][k * T + t0:k * T + t0 + tn, :]
                                   ).then_inc(sem(f"y12_in{t}"), 16)

        pool.memset(fill[:, :], OOB).then_inc(sem("fill"), 1)
        pool.wait_ge(sem("fill"), 1)
        for L in range(2):
            pool.dma_start(lists[L].rearrange("(c r) v -> c (r v)", r=P), fill[:, :]
                           ).then_inc(sem("list_clear"), 16)
        pool.wait_ge(sem("ptab_in"), 16)
        for c in range(8):
            if c < 7:
                pool.wait_ge(sem("slot_free"), c + 1)
            else:
                pool.wait_ge(sem("rows_free"), 1)
            for b in range(4):
                for pg in range(2):
                    at = (4 * (c // 4) + b) * PAGES + 2 * (c % 4) + pg
                    page = pool.value_load(ptab[0:1, at:at + 1], min_val=0, max_val=io["n_phys"] - 1)
                    pool.dma_start(ring(c % 7, (2 * b + pg) * KV, KV),
                                   io["row_pages"][bass.ds(page, 1)].rearrange("a p n -> (a p) n")
                                   ).then_inc(sem(f"rows_full{c // 4}"), 16)
        moe(0)
        moe(1)

    @block.scalar
    def _(act):
        def square(name, src, sq, k):
            if H_STAGE.get(name):
                act.wait_ge(sem("h_upd"), 8 * (H_STAGE[name] - 1) + k + 1)
            nc.scalar.activation(sq[:, k, :], src[:, k, :], ACT.Square).then_inc(sem("sq"), 1)

        def root(name, feats):
            n = N_IDX[name]
            act.wait_ge(sem("ss_ps"), n + 1)
            if n >= 1:
                act.wait_ge(sem("hn"), N_BASE[name])
            nc.scalar.activation(std_t[:, :], bank(7, T), ACT.Sqrt, bias=eps[:, 0:1],
                                 scale=1.0 / feats).then_inc(sem("std"), 1)

        def norm(name, src, sq, feats, k0=0):
            for k in range(k0, N_K[name]):
                if k == N_K[name] - 1:
                    nc.scalar.activation(eps[:, 2:3], eps[:, 0:1], ACT.Sqrt)
                square(name, src, sq, k)
            root(name, feats)

        act.dma_start(par[:, :], io["par"]).then_inc(sem("const_in"), 16)
        act.dma_start(const[:, :], io["const"]).then_inc(sem("const_in"), 16)
        act.dma_start(aconst, io["aconst"]).then_inc(sem("aconst_in"), 16)
        act.dma_start(ptab[:, :], io["ptab"]).then_inc(sem("ptab_in"), 16)
        act.dma_start(w_r[:, :, :, :], io["w_r"]).then_inc(sem("wr_in"), 16)
        act.dma_start(b_r[:, :, :], io["b_r"]).then_inc(sem("wr_in"), 16)

        act.wait_ge(sem("x_in"), 16)
        act.wait_ge(sem("eps"), 2)
        norm("mix0", h_t, hn_t, D)
        for m in range(5):
            act.wait_ge(sem("a_ps"), m + 1)
            dst = cq[:, m, :] if m < 3 else ckvT[:, m - 3, :]
            nc.scalar.activation(dst, bank(m, T), ACT.Copy).then_inc(sem("a_sb"), 1)
            if m == 2:
                act.wait_ge(sem("a_sb"), 3)
                norm("cq", cq, sq_a, QL)
        act.wait_ge(sem("a_sb"), 5)
        norm("ckv", ckvT, sq_c, KV)
        act.wait_ge(sem("hn"), N_BASE["ckv"] + 2)
        act.dma_start(io["ckv_out"], ckvT[:, :, :]).then_inc(sem("out"), 16)
        act.wait_ge(sem("kr"), 1)
        act.dma_start(io["kr_out"], krT).then_inc(sem("out"), 16)
        for h in range(H):
            act.wait_ge(sem("qn_ps"), h + 1)
            nc.scalar.activation(qn[:, h, :], bank(2 + h % 2, T), ACT.Copy).then_inc(sem("qn_sb"), 1)
        for h in range(H):
            act.wait_ge(sem("ql_ps"), 2 * h + 1)
            nc.scalar.activation(ql[:, h, 0, :], bank((2 * h) % 4, T), ACT.Copy).then_inc(sem("ql_a"), 1)

        def exp_prompt(h):
            u = h % 2
            act.wait_ge(sem("nmax"), h + 1)
            if h >= 2:
                act.wait_ge(sem("pt_ps"), h - 1)
            nc.scalar.activation(p_p[:, u, 0:128], s_p[:, u, 0:128], ACT.Exp, bias=nmx[:, u, 0:1],
                                 scale=SCALE, accum_out=lsum[:, u, 0:1])
            nc.scalar.activation(p_p[:, u, 128:384], s_p[:, u, 128:384], ACT.Exp, bias=nmx[:, u, 1:2],
                                 scale=SCALE, accum_out=lsum[:, u, 1:2]).then_inc(sem("exp"), 1)

        def copy_pt(h):
            act.wait_ge(sem("pt_ps"), h + 1)
            nc.scalar.activation(pt_p[:, :], bank(2, 384), ACT.Copy).then_inc(sem("pt_sb"), 1)

        def exp_sample(r):
            act.wait_ge(sem("s_nmax"), r + 1)
            if r == 0:
                act.wait_ge(sem("list_clear"), 32)
            nc.scalar.activation(p_s[:, 0:PAST].rearrange("p (b n) -> p b n", b=2), ps[:, 4:6, :], ACT.Exp, bias=s_nmx,
                                 scale=SCALE, accum_out=s_l[:, 0:1])
            nc.scalar.activation(p_s[:, PAST:PAST + NS_], snew, ACT.Exp, bias=s_nmx, scale=SCALE,
                                 accum_out=s_l[:, 1:2]).then_inc(sem("s_exp"), 1)

        def copy_pts(r):
            act.wait_ge(sem("s_pt_ps"), r + 1)
            nc.scalar.activation(pt_s[:, 0:4, :].rearrange("p g r -> p (g r)"), bank(4), ACT.Copy
                                 ).then_inc(sem("s_pt_a"), 1)

        exp_prompt(0)
        for h in range(H):
            if h + 1 < H:
                exp_prompt(h + 1)
            copy_pt(h)
            if h == 3:
                copy_pts(0)
            if h in (2, 7):
                exp_sample(h // 4)
        copy_pts(1)
        for h in range(0, H, 2):
            act.wait_ge(sem("o_ps"), h + 1)
            nc.scalar.activation(oT[:, h, :], bank(h % 4, T), ACT.Copy).then_inc(sem("o_a"), 1)

        def moe(L):
            if L == 0:
                act.wait_ge(sem("out"), 32)
            norm(f"ffn{L}", h_t, hn_t, D)
            act.wait_ge(sem("h_upd"), 8 * (1 if L == 0 else 4))
            act.dma_start(pT, io["p"][:, L]).then_inc(sem("pT_in"), 16)
            for t, (t0, tn) in enumerate(TOK):
                act.wait_ge(sem("hr_ps"), 3 * L + t + 1)
                b0 = 2 + 2 * (t % 2)
                nc.scalar.activation(hn_tok[0:tn, t, :], ps[0:tn, b0:b0 + 2, :].rearrange("p b n -> p (b n)"), ACT.Copy).then_inc(sem("hr_a"), 1)
                act.wait_ge(sem("hr_a"), 3 * L + t + 1)
                act.dma_start(hn_rows[L][t0:t0 + tn, :], hn_tok[0:tn, t, :]).then_inc(sem("hn_rows"), 16)
            act.wait_ge(sem("dx"), L + 1)
            nc.scalar.activation(ex, dx, ACT.Exp).then_inc(sem("ex"), 1)
            for m in range(KD):
                act.wait_ge(sem("prj_ps"), 8 * L + m + 1)
                nc.scalar.activation(prj[:, m, :], bank(4 + m % 4, T), ACT.Copy).then_inc(sem("prj"), 1)

            def pair(i, b):
                act.wait_ge(sem(f"x_ps{L}"), i * 2 + (b + 1))
                nc.scalar.activation(xT[:, 0:4, :].rearrange("p k s -> p (k s)"), bank(0), ACT.Copy).then_inc(sem(f"xT_a{L}"), 1)
                act.wait_ge(sem(f"h_ps{L}"), i * 2 + (b + 1))
                nc.scalar.activation(sil, ps[:, 2 + b, 0:FH], ACT.Silu).then_inc(sem(f"sil{L}"), 1)
                act.wait_ge(sem(f"aT_ps{L}"), i * 2 + (b + 1))
                nc.scalar.activation(aT.rearrange("p k s -> p (k s)"), ps[:, 4, 0:256], ACT.Copy).then_inc(sem(f"aT{L}"), 1)
                act.wait_ge(sem(f"y_ps{L}"), i * 2 + (b + 1))
                act.wait_ge(sem(f"y_free{L}"), i * 2 + (b + 1))
                nc.scalar.activation(y_sb[:, b, 0:512], bank(5), ACT.Copy).then_inc(sem(f"y_a{L}"), 1)

            act.sem_inc(sem(f"y_a{L}"), 1)
            with act.Fori(0, PAIRS // 2) as i:
                for b in range(2):
                    pair(i, b)
            act.wait_ge(sem("cnt"), L + 1)
            most = act.value_load(cnt_i[0:1, L:L + 1], min_val=0, max_val=T)
            with act.If(most > WIN):
                with act.Fori(PAIRS // 2, PASSES * PAIRS // 2) as i:
                    for b in range(2):
                        pair(i, b)
            for t, (t0, tn) in enumerate(TOK):
                act.wait_ge(sem(f"y12_in{t}"), 32 * L + 32)
                if t == 0:
                    act.wait_ge(sem("gates"), L + 1)
                nc.scalar.activation(y12[0:tn, 0, t, :], y12[0:tn, 0, t, :], ACT.Copy, scale=gate_w[0:tn, t, 0:1]
                                     ).then_inc(sem("comb_a"), 1)
            norm(f"ple{L}", h_t, hn_t, D)
            if L == 0:
                act.wait_ge(sem("h_upd"), 16)
                for name, dst in (("ws", wsT), ("wss", wsS), ("bs", bs)):
                    act.dma_start(dst, io[name]).then_inc(sem("ws_in"), 16)
            for m in range(KD):
                if m >= 2:
                    square(NEXT[L], h_t, prj, m - 2)
                act.wait_ge(sem("pg_ps"), 8 * L + m + 1)
                if m >= 4:
                    act.wait_ge(sem("h_upd"), 8 * (2 if L == 0 else 5) + m - 3)
                nc.scalar.activation(sg[:, m % 4, :], bank(m % 4, T), ACT.Sigmoid).then_inc(sem("pg_sig"), 1)
            norm(NEXT[L], h_t, prj, D, KD - 2)

        moe(0)

        for t in range(FT):
            act.wait_ge(sem("z_ps"), t + 1)
            if t >= 2:
                act.wait_ge(sem("vt_ps"), t - 1)
            nc.scalar.activation(vT[:, t % 2, :], bank(t % 4, T), ACT.Gelu_apprx_tanh,
                                 bias=par[:, B_IN + FT + t:B_IN + FT + t + 1]).then_inc(sem("z_sb"), 1)
        for t in range(FT):
            if t == 3:
                act.wait_ge(sem("v_mv"), 3)
                nc.scalar.activation(vst[:, 0:2, 0:1], mv[:, 0:2, 1:2], ACT.Sqrt, bias=eps[:, 1:2]).then_inc(sem("v_std"), 1)
                nc.scalar.activation(vst[0:NS_, 2, 0:1], mv[0:NS_, 2, 1:2], ACT.Sqrt, bias=eps[0:NS_, 1:2]).then_inc(sem("v_std"), 1)
            act.wait_ge(sem("z_ps"), FT + t + 1)
            nc.scalar.activation(uT[:, t, :], bank(t % 4, T), ACT.Gelu_apprx_tanh,
                                 bias=par[:, B_IN + t:B_IN + t + 1]).then_inc(sem("z_sb"), 1)
        act.wait_ge(sem("vs"), 1)
        act.dma_start(io["vs_out"], vsT).then_inc(sem("vs_out"), 16)
        act.wait_ge(sem("vs_out"), 16)
        moe(1)
        for k in range(KD):
            act.wait_ge(sem("hn"), N_BASE["fin"] + k + 1)
            act.dma_start(io["y_out"][:, k, :], hn_t[:, k, :]).then_inc(sem("out"), 16)
        act.wait_ge(sem("out"), 16 * (2 + KD))

    @block.vector
    def _(dve):
        done = [0]

        def link(ins):
            done[0] += 1
            ins.then_inc(sem("dve_step"), 1)
            dve.wait_ge(sem("dve_step"), done[0])

        def norm(name, src, dst, g0):
            dve.wait_ge(sem("std"), N_IDX[name] + 1)
            if N_IDX[name]:
                dve.wait_ge(sem("hn"), N_BASE[name])
            link(nc.vector.reciprocal(rstd_t[:, :], std_t[:, :]))
            for k in range(N_K[name]):
                nc.vector.scalar_tensor_tensor(out=dst[:, k, :], in0=src[:, k, :],
                                               scalar=par[:, g0 + k:g0 + k + 1], in1=rstd_t[:, :],
                                               op0=ALU.mult, op1=ALU.mult).then_inc(sem("hn"), 1)

        def add_h(k, what):
            nc.vector.tensor_tensor(h_t[:, k, :], h_t[:, k, :], what, ALU.add).then_inc(sem("h_upd"), 1)

        nc.vector.memset(eps[:, 0:1], 1e-6).then_inc(sem("eps"), 1)
        nc.vector.memset(eps[:, 1:2], 1e-5).then_inc(sem("eps"), 1)
        dve.wait_ge(sem("const_in"), 32)
        norm("mix0", h_t, hn_t, G_MIX[0])

        dve.wait_ge(sem("aconst_in"), 16)
        cos, sin = aconst[:, C_COS:C_COS + T], aconst[:, C_SIN:C_SIN + T]
        norm("cq", cq, cq, G_Q)
        norm("ckv", ckvT, ckvT, G_KV)
        dve.wait_ge(sem("a_ps"), 7)
        link(nc.vector.tensor_tensor(rt[0:RO, 0, :], ps[0:RO, 5, 0:T], cos[0:RO], ALU.mult))
        link(nc.vector.tensor_tensor(rt[0:RO, 1, :], ps[0:RO, 6, 0:T], sin[0:RO], ALU.mult))
        nc.vector.tensor_tensor(krT, rt[0:RO, 0, :], rt[0:RO, 1, :], ALU.add).then_inc(sem("kr"), 1)
        dve.wait_ge(sem("kr"), 1)
        dve.wait_ge(sem("ckt_ps"), 1)
        nc.vector.tensor_copy(ckt[:, 0:2, :].rearrange("p t c -> p (t c)"), bank(0)).then_inc(sem("ckt"), 1)
        nc.vector.tensor_copy(ckt[0:NS_, 2, :], ps[0:NS_, 1, 0:KV]).then_inc(sem("ckt"), 1)
        for p in range(H // 2):
            b0 = 4 + 2 * (p % 2)
            dve.wait_ge(sem("qr_ps"), p + 1)
            link(nc.vector.tensor_tensor(rt[:, 0, :], bank(b0, T), cos, ALU.mult))
            link(nc.vector.tensor_tensor(rt[:, 1, :], bank(b0 + 1, T), sin, ALU.mult))
            link(nc.vector.tensor_tensor(qr[:, 2 * p, :], rt[0:RO, 0, :], rt[0:RO, 1, :], ALU.add))
            nc.vector.tensor_tensor(qr[:, 2 * p + 1, :], rt[RO:P, 0, :], rt[RO:P, 1, :], ALU.add).then_inc(sem("qr"), 1)
            dve.wait_ge(sem("qr"), p + 1)
        for h in range(H):
            dve.wait_ge(sem("ql_ps"), 2 * h + 2)
            nc.vector.tensor_copy(ql[:, h, 1, :], bank((2 * h + 1) % 4, T)).then_inc(sem("ql_d"), 1)

        dve.wait_ge(sem("ql_a"), H)
        dve.wait_ge(sem("ql_d"), H)
        for c in range(3):
            a, n = (ql[:, :, c, NP_:T], P) if c < 2 else (qr[:, :, NP_:T], RO)
            nc.vector.tensor_copy(qs[0:n, c].rearrange("p b (h s) -> p b h s", h=H),
                                  a.rearrange("p h (b s) -> p b h s", b=DEC_B)).then_inc(sem("qs"), 1)

        def max_prompt(h):
            u = h % 2
            dve.wait_ge(sem("sc_ps"), h + 1)
            nc.vector.tensor_tensor(s_p[:, u, :], bank(u, 384), aconst[:, C_MSK:C_MSK + 384], ALU.add).then_inc(sem("masked"), 1)
            dve.wait_ge(sem("masked"), h + 1)
            link(nc.vector.tensor_reduce(mx[:, 0:1], s_p[:, u, 0:128], AX.X, ALU.max))
            link(nc.vector.tensor_reduce(mx[:, 1:2], s_p[:, u, 128:384], AX.X, ALU.max))
            nc.vector.tensor_scalar(nmx[:, u, :], mx, -SCALE, None, ALU.mult).then_inc(sem("nmax"), 1)

        def norm_prompt(h):
            u = h % 2
            dve.wait_ge(sem("exp"), h + 1)
            link(nc.vector.reciprocal(rl[:, u, :], lsum[:, u, :]))
            link(nc.vector.tensor_scalar(p_p[:, u, 0:128], p_p[:, u, 0:128], rl[:, u, 0:1], None, ALU.mult))
            nc.vector.tensor_scalar(p_p[:, u, 128:384], p_p[:, u, 128:384], rl[:, u, 1:2], None, ALU.mult).then_inc(sem("p_n"), 1)

        def take_prompt(h):
            dve.wait_ge(sem("pv_ps"), h + 1)
            nc.vector.tensor_copy(ql[:, h, :, 0:NP_], ps[:, 3, :].rearrange("p (c t) -> p c t", c=2)).then_inc(sem("ol"), 1)

        def max_sample(r):
            dve.wait_ge(sem("s_ps"), r + 1)
            link(nc.vector.tensor_tensor(snew, ps[:, 6, 0:NS_], aconst[:, C_SMSK + NS_ * r:C_SMSK + NS_ * r + NS_], ALU.add))
            link(nc.vector.tensor_reduce(s_mx[:, 0:1], ps[:, 4:6, :], AX.XY, ALU.max))
            link(nc.vector.tensor_reduce(s_mx[:, 1:2], snew, AX.X, ALU.max))
            link(nc.vector.tensor_tensor(s_mx[:, 0:1], s_mx[:, 0:1], s_mx[:, 1:2], ALU.max))
            nc.vector.tensor_scalar(s_nmx, s_mx[:, 0:1], -SCALE, None, ALU.mult).then_inc(sem("s_nmax"), 1)

        def norm_sample(r):
            dve.wait_ge(sem("s_exp"), r + 1)
            link(nc.vector.tensor_tensor(s_l[:, 0:1], s_l[:, 0:1], s_l[:, 1:2], ALU.add))
            link(nc.vector.reciprocal(s_l[:, 1:2], s_l[:, 0:1]))
            nc.vector.tensor_scalar(p_s, p_s, s_l[:, 1:2], None, ALU.mult).then_inc(sem("s_pn"), 1)

        def take_pts(r):
            dve.wait_ge(sem("s_pt_ps"), r + 1)
            nc.vector.tensor_copy(pt_s[:, 4:8, :].rearrange("p g r -> p (g r)"), bank(5)).then_inc(sem("s_pt_d"), 1)
            nc.vector.tensor_copy(pt_s[0:NS_, 8, :], ps[0:NS_, 6, 0:P]).then_inc(sem("s_pt_d"), 1)

        def take_ola(r):
            dve.wait_ge(sem("s_o_ps"), r + 1)
            nc.vector.tensor_copy(ola_s, bank(7, KV)).then_inc(sem("s_ola"), 1)

        def take_ol(r):
            dve.wait_ge(sem("s_ot_ps"), r + 1)
            for c in range(2):
                nc.vector.tensor_copy(
                    ql[:, :, c, NP_ + 16 * r:NP_ + 16 * r + 16].rearrange("p h (b s) -> p b h s", b=4),
                    ps[:, 6, 128 + 128 * c:256 + 128 * c].rearrange("p (b h s) -> p b h s", b=4, h=H)
                ).then_inc(sem("s_ol"), 1)

        max_prompt(0)
        for h in range(H):
            if h == 6:
                take_ol(0)
            if h + 1 < H:
                max_prompt(h + 1)
            norm_prompt(h)
            if h == 3:
                norm_sample(0)
            if h == 5:
                take_ola(0)
            if h == 7:
                max_sample(1)
            take_prompt(h)
            if h == 2:
                max_sample(0)
            if h == 3:
                take_pts(0)
        norm_sample(1)
        take_pts(1)
        take_ola(1)
        take_ol(1)
        for h in range(1, H, 2):
            dve.wait_ge(sem("o_ps"), h + 1)
            nc.vector.tensor_copy(oT[:, h, :], bank(h % 4, T)).then_inc(sem("o_d"), 1)
        for m in range(KD):
            dve.wait_ge(sem("h_part"), m + 1)
            add_h(m, bank(WO_BANK[m % 4], T))

        io3 = const[:, C_IOTA:C_IOTA + EPG]

        def bc(a, shape):
            return a.to_broadcast(shape)

        def first_of(vals, top, n, tmp, out):
            link(nc.vector.tensor_tensor(tmp, vals, bc(top.unsqueeze(2), [P, 3, n]), ALU.is_lt))
            link(nc.vector.scalar_tensor_tensor(out=tmp, in0=tmp, scalar=100.0,
                                                in1=bc(io3[:, 0:n].unsqueeze(1), [P, 3, n]),
                                                op0=ALU.mult, op1=ALU.add))
            link(nc.vector.tensor_reduce(out, tmp, AX.X, ALU.min))

        def moe(L):
            norm(f"ffn{L}", h_t, hn_t, G_FFN[L])
            dve.wait_ge(sem("wr_in"), 32)
            link(nc.vector.memset(lgt[:, 2, :], 0.0))
            dve.wait_ge(sem("lg_ps"), L + 1)
            pl = ps[:, 0, 0:108].rearrange("p (t n) -> p t n", t=3)
            link(nc.vector.tensor_tensor(lgt[:, 0:2, :], pl[:, 0:2, :], bc(b_r[:, L, :].unsqueeze(1), [P, 2, 36]), ALU.add))
            link(nc.vector.tensor_tensor(lgt[0:NS_, 2, :], pl[0:NS_, 2, :], b_r[0:NS_, L, :], ALU.add))
            link(nc.vector.tensor_reduce(gmx, lg, AX.X, ALU.max))
            dx4 = dx[:, 0:12].rearrange("p (t g) -> p t g", t=3)
            link(nc.vector.tensor_tensor(dx4, lg, bc(gmx.unsqueeze(2), [P, 3, G]), ALU.subtract))
            first_of(lg, gmx, G, t4, gid)
            link(nc.vector.tensor_tensor(og, bc(io3[:, 0:G].unsqueeze(1), [P, 3, G]), bc(gid.unsqueeze(2), [P, 3, G]), ALU.is_equal))
            link(nc.vector.tensor_tensor(t32, le, bc(og.unsqueeze(3), [P, 3, G, EPG]), ALU.mult))
            link(nc.vector.tensor_reduce(leg, t32.rearrange("p t g j -> p t j g"), AX.X, ALU.add))
            for k, src in ((0, leg), (1, leg2)):
                link(nc.vector.tensor_reduce(mk[:, k, :], src, AX.X, ALU.max))
                first_of(src, mk[:, k, :], EPG, t8, ik[:, k, :])
                link(nc.vector.tensor_tensor(oh[:, k], bc(io3.unsqueeze(1), [P, 3, EPG]), bc(ik[:, k, :].unsqueeze(2), [P, 3, EPG]), ALU.is_equal))
                if k == 0:
                    link(nc.vector.scalar_tensor_tensor(out=leg2, in0=oh[:, 0], scalar=NEG, in1=leg, op0=ALU.mult, op1=ALU.add))
                link(nc.vector.tensor_tensor(ek[:, k].rearrange("p t (g j) -> p t g j", g=G),
                                             bc(og.unsqueeze(3), [P, 3, G, EPG]),
                                             bc(oh[:, k].unsqueeze(2), [P, 3, G, EPG]), ALU.mult))
            nc.vector.tensor_tensor(sel, ek[:, 0], ek[:, 1], ALU.add).then_inc(sem("sel"), 1)
            nc.vector.tensor_tensor(dx[:, 12:15], mk[:, 1, :], mk[:, 0, :], ALU.subtract).then_inc(sem("dx"), 1)
            dve.wait_ge(sem("ex"), L + 1)
            link(nc.vector.tensor_reduce(gs, ex[:, 0:12].rearrange("p (t g) -> p t g", t=3), AX.X, ALU.add))
            link(nc.vector.tensor_scalar(den, ex[:, 12:15], 1.0, None, ALU.add))
            link(nc.vector.tensor_tensor(den, den, gs, ALU.mult))
            link(nc.vector.reciprocal(gate_w[:, :, 0], den))
            nc.vector.tensor_tensor(gate_w[:, :, 1], gate_w[:, :, 0], ex[:, 12:15], ALU.mult).then_inc(sem("gates"), 1)
            dve.wait_ge(sem("rank_ps"), L + 1)
            t32f = t32.rearrange("p t g j -> p t (g j)")
            for k in range(2):
                link(nc.vector.tensor_tensor(t32f, ek[:, k], ps[:, 1, 0:96].rearrange("p (t e) -> p t e", t=3), ALU.mult))
                link(nc.vector.tensor_reduce(rk[:, k, :], t32f, AX.X, ALU.add))
            link(nc.vector.tensor_scalar(win, rk, float(WIN), None, ALU.is_ge))
            for j in range(2, PASSES):
                link(nc.vector.scalar_tensor_tensor(out=win, in0=rk, scalar=float(WIN * j), in1=win, op0=ALU.is_ge, op1=ALU.add))
            link(nc.vector.scalar_tensor_tensor(out=row, in0=win, scalar=float(WIN * NE - WIN), in1=rk, op0=ALU.mult, op1=ALU.add))
            link(nc.vector.scalar_tensor_tensor(out=row, in0=ik, scalar=float(WIN), in1=row, op0=ALU.mult, op1=ALU.add))
            link(nc.vector.scalar_tensor_tensor(out=row, in0=bc(gid.unsqueeze(1), [P, 2, 3]), scalar=float(WIN * EPG), in1=row, op0=ALU.mult, op1=ALU.add))
            link(nc.vector.tensor_tensor(row, row, bc(const[:, C_INV:C_INV + 3].unsqueeze(1), [P, 2, 3]), ALU.add))
            nc.vector.tensor_copy(row_i, row).then_inc(sem("row_i"), 1)
            dve.wait_ge(sem("total_ps"), L + 1)
            link(nc.vector.tensor_reduce(cmx, ps[:, 3, 0:32], AX.X, ALU.max))
            nc.vector.tensor_copy(cnt_i[:, L:L + 1], cmx).then_inc(sem("cnt"), 1)
            dve.wait_ge(sem("lst_ps"), L + 1)
            nc.vector.tensor_copy(slots[:, :, 0], ps[:, 2, 0:COLS])
            nc.vector.tensor_copy(slots[:, :, 1], ps[:, 2, 128:128 + COLS]).then_inc(sem("slots"), 1)

            def pair(i, b):
                dve.wait_ge(sem(f"x_ps{L}"), i * 2 + (b + 1))
                nc.vector.tensor_copy(xT[:, 4:8, :].rearrange("p k s -> p (k s)"), bank(1)).then_inc(sem(f"xT_d{L}"), 1)
                dve.wait_ge(sem(f"sil{L}"), i * 2 + (b + 1))
                nc.vector.tensor_tensor(act_a, sil, ps[:, 2 + b, FH:2 * FH], ALU.mult).then_inc(sem(f"a{L}"), 1)
                dve.wait_ge(sem(f"y_ps{L}"), i * 2 + (b + 1))
                dve.wait_ge(sem(f"y_free{L}"), i * 2 + (b + 1))
                nc.vector.tensor_copy(y_sb[:, b, 512:1024], bank(6)).then_inc(sem(f"y_d{L}"), 1)

            dve.sem_inc(sem(f"y_d{L}"), 1)
            with dve.Fori(0, PAIRS // 2) as i:
                for b in range(2):
                    pair(i, b)
            dve.wait_ge(sem("cnt"), L + 1)
            most = dve.value_load(cnt_i[0:1, L:L + 1], min_val=0, max_val=T)
            with dve.If(most > WIN):
                with dve.Fori(PAIRS // 2, PASSES * PAIRS // 2) as i:
                    for b in range(2):
                        pair(i, b)
            for t, (t0, tn) in enumerate(TOK):
                dve.wait_ge(sem(f"y12_in{t}"), 32 * L + 32)
                dve.wait_ge(sem("comb_a"), 3 * L + t + 1)
                nc.vector.scalar_tensor_tensor(out=y12[0:tn, 0, t, :], in0=y12[0:tn, 1, t, :], scalar=gate_w[0:tn, t, 1:2],
                                               in1=y12[0:tn, 0, t, :], op0=ALU.mult, op1=ALU.add).then_inc(sem("comb"), 1)
            for k in range(KD):
                dve.wait_ge(sem("h_part"), 8 + 16 * L + k + 1)
                add_h(k, bank(k % 4, T))
            norm(f"ple{L}", h_t, hn_t, G_PLE[L])
            if L == 0:
                dve.wait_ge(sem("ws_in"), 48)
                nc.vector.tensor_tensor(wsT, wsT, bc(const[:, C_WM:C_WM + P].unsqueeze(1), [P, 8, P]), ALU.mult).then_inc(sem("ws_m"), 1)
                nc.vector.tensor_tensor(wsS, wsS, bc(const[0:NS_, C_WSM:C_WSM + NS_].unsqueeze(1), [NS_, 8, NS_]), ALU.mult).then_inc(sem("ws_m"), 1)
            for m in range(KD):
                if m == 3 and L == 0:
                    dve.wait_ge(sem("rs_ps"), 1)
                    nc.vector.tensor_copy(rs[:, :, 0:P], ps[:, 5:7, :].rearrange("p b (g r) -> p (b g) r", g=4)).then_inc(sem("rs"), 1)
                    nc.vector.tensor_copy(rs[:, :, P:160], ps[:, 4, 0:256].rearrange("p (g r) -> p g r", g=8)).then_inc(sem("rs"), 1)
                dve.wait_ge(sem("pg_sig"), 8 * L + m + 1)
                nc.vector.tensor_tensor(sg[:, m % 4, :], sg[:, m % 4, :], prj[:, m, :], ALU.mult).then_inc(sem("pg_in"), 1)
                dve.wait_ge(sem("pg_in"), 8 * L + m + 1)
                nc.vector.tensor_tensor(h_t[:, m, :], h_t[:, m, :], sg[:, m % 4, :], ALU.add).then_inc(sem("h_upd"), 1)

        moe(0)

        norm("mix1", h_t, hn_t, G_MIX[1])
        for t in range(FT):
            dve.wait_ge(sem("vt_ps"), t + 1)
            nc.vector.tensor_copy(v_tok[:, 0:2, t * P:(t + 1) * P], ps[:, 4 + t % 2, 0:256].rearrange("p (t f) -> p t f", t=2)).then_inc(sem("v_sb"), 1)
            nc.vector.tensor_copy(v_tok[0:NS_, 2, t * P:(t + 1) * P], ps[0:NS_, 4 + t % 2, 256:384]).then_inc(sem("v_sb"), 1)
        dve.wait_ge(sem("v_sb"), 2 * FT)
        link(nc.vector.memset(vst[:, :, :], 1.0))
        for t, (t0, tn) in enumerate(TOK):
            for c in range(6):
                ins = nc.vector.bn_stats(bst[0:tn, 36 * t + 6 * c:36 * t + 6 * c + 6], v_tok[0:tn, t, 512 * c:512 * c + 512])
            link(ins)
            nc.vector.bn_aggr(mv[0:tn, t, :], bst[0:tn, 36 * t:36 * t + 36]).then_inc(sem("v_mv"), 1)
        dve.wait_ge(sem("v_std"), 2)
        link(nc.vector.reciprocal(vst[:, :, 1], vst[:, :, 0]))
        for t, (t0, tn) in enumerate(TOK):
            nc.vector.tensor_scalar(v_tok[0:tn, t, :], v_tok[0:tn, t, :], mv[0:tn, t, 0:1], vst[0:tn, t, 1:2],
                                    ALU.subtract, ALU.mult).then_inc(sem("v_n"), 1)

        for t in range(FT):
            g = t // 3
            gv, bv = par[:, G_V + t:G_V + t + 1], par[:, B_V + t:B_V + t + 1]
            if t:
                dve.wait_ge(sem("g_sb"), t)
            for c0, cn, r0 in ((0, P, 0), (P, P, 0), (2 * P, NS_, P)):
                ins = nc.vector.scalar_tensor_tensor(out=tm[:, c0:c0 + cn], in0=rs[:, g, r0:r0 + cn], scalar=bv,
                                                     in1=bs[:, g, r0:r0 + cn], op0=ALU.mult, op1=ALU.add)
            link(ins)
            dve.wait_ge(sem("sp_ps"), t + 1)
            link(nc.vector.scalar_tensor_tensor(out=sr, in0=bank(6 + t % 2, T), scalar=gv, in1=tm, op0=ALU.mult, op1=ALU.add))
            dve.wait_ge(sem("z_sb"), FT + t + 1)
            nc.vector.tensor_tensor(uT[:, t, :], uT[:, t, :], sr, ALU.mult).then_inc(sem("g_sb"), 1)
        dve.wait_ge(sem("vs_ps"), 1)
        vps = ps[:, 4:6, :].rearrange("p b n -> p (b n)")[:, 0:FT * NS_].rearrange("p (f t) -> p f t", t=NS_)
        link(nc.vector.tensor_tensor(vsT, vps, bc(par[:, G_V:G_V + FT].unsqueeze(2), [P, FT, NS_]), ALU.mult))
        nc.vector.tensor_tensor(vsT, vsT, bc(par[:, B_V:B_V + FT].unsqueeze(2), [P, FT, NS_]), ALU.add).then_inc(sem("vs"), 1)
        for m in range(KD):
            dve.wait_ge(sem("h_part"), 16 + m + 1)
            add_h(m, bank(m % 4, T))
        moe(1)
        norm("fin", h_t, hn_t, G_FIN)

    @block.tensor
    def _(pe):
        mm = nc.tensor.matmul

        def sum_sq(name, sq, k):
            n = N_IDX[name]
            if n and k == 0:
                pe.wait_ge(sem("std"), n)
            pe.wait_ge(sem("sq"), N_BASE[name] + k + 1)
            last = mm(bank(7, T), ones, sq[:, k, :], start=(k == 0), stop=(k == N_K[name] - 1))
            if k == N_K[name] - 1:
                last.then_inc(sem("ss_ps"), 1)
            else:
                free_with(last)

        def norm(name, sq, k0=0):
            for k in range(k0, N_K[name]):
                sum_sq(name, sq, k)

        pe.sem_inc(sem("key_free"), 2)
        pe.wait_ge(sem("const_in"), 32)
        norm("mix0", hn_t)
        wait_slots(pe, S_IN, S_IN + 3)
        at = 0
        for m, mn in enumerate([P] * 5 + [RO] * 2):
            for k in range(KD):
                if m == 0:
                    pe.wait_ge(sem("hn"), N_BASE["mix0"] + k + 1)
                last = mm(ps[0:mn, m, 0:T], ring(S_IN, at, mn), hn_t[:, k, :], start=(k == 0), stop=(k == KD - 1))
                at += mn
            last.then_inc(sem("a_ps"), 1)
            if m == 3:
                norm("cq", sq_a)
        owe(3)
        norm("ckv", sq_c)
        pe.wait_ge(sem("a_sb"), 5)
        pe.wait_ge(sem("hn"), N_BASE["ckv"] + 2)
        for t, (t0, tn) in enumerate(TOK):
            for c in range(2):
                last = nc.tensor.transpose(ps[0:tn, t // 2, (t % 2) * KV + c * P:(t % 2) * KV + c * P + P],
                                           ckvT[:, c, t0:t0 + tn], ident)
        last.then_inc(sem("ckt_ps"), 1)
        wait_slots(pe, S_QB, S_QB + 3)

        def q_tile(j, b):
            for k in range(3):
                last = mm(bank(b, T), ring(S_QB, j * 384 + k * P, P), cq[:, k, :], start=(k == 0), stop=(k == 2))
            return last

        for h in range(H):
            if h >= 2:
                pe.wait_ge(sem("qn_sb"), h - 1)
            q_tile(h, 2 + h % 2).then_inc(sem("qn_ps"), 1)
        pe.wait_ge(sem("kr"), 1)
        pe.wait_ge(sem("std"), N_IDX["ckv"] + 1)
        for p in range(H // 2):
            if p >= 2:
                pe.wait_ge(sem("qr"), p - 1)
            q_tile(H + 2 * p, 4 + 2 * (p % 2))
            q_tile(H + 2 * p + 1, 5 + 2 * (p % 2)).then_inc(sem("qr_ps"), 1)
        owe(3)
        wait_slots(pe, S_UK, S_UK + 1)
        pe.wait_ge(sem("ckt"), 2)
        for h in range(H):
            pe.wait_ge(sem("qn_sb"), h + 1)
            for c in range(2):
                if h >= 2:
                    pe.wait_ge(sem("ql_a" if c == 0 else "ql_d"), h - 1)
                mm(bank((2 * h + c) % 4, T), ring(S_UK, h * KV + c * P, P), qn[:, h, :], start=True, stop=True).then_inc(sem("ql_ps"), 1)
            if h == 0:
                pe.wait_ge(sem("qn_sb"), H)
        owe(1)
        pe.wait_ge(sem("ql_a"), H)
        pe.wait_ge(sem("ql_d"), H)
        pe.wait_ge(sem("qr"), H // 2)

        def scores(h):
            u = h % 2
            if h >= 2:
                pe.wait_ge(sem("masked"), h - 1)
            for c0, q0, kn in ((0, 0, P), (P, P, NP_)):
                free_with(mm(ps[:, u, c0:c0 + kn], ql[:, h, 0, q0:q0 + P], ckvT[:, 0, 0:kn], start=True, stop=False))
                mm(ps[:, u, c0:c0 + kn], ql[:, h, 1, q0:q0 + P], ckvT[:, 1, 0:kn], start=False, stop=False)
                last = mm(ps[:, u, c0:c0 + kn], qr[:, h, q0:q0 + P], krT[:, 0:kn], start=False, stop=True)
            last.then_inc(sem("sc_ps"), 1)

        def turn_p(h):
            pe.wait_ge(sem("p_n"), h + 1)
            for j in range(3):
                last = nc.tensor.transpose(ps[:, 2, j * P:(j + 1) * P], p_p[:, h % 2, j * P:(j + 1) * P], ident)
            last.then_inc(sem("pt_ps"), 1)

        def apply_p(h):
            pe.wait_ge(sem("pt_sb"), h + 1)
            if h >= 1:
                pe.wait_ge(sem("ol"), h)
            for c in range(2):
                mm(ps[:, 3, c * NP_:(c + 1) * NP_], ckt[:, 0, c * P:(c + 1) * P], pt_p[:, 0:NP_], start=True, stop=False)
                last = mm(ps[:, 3, c * NP_ + P:(c + 1) * NP_], ckt[:, 1, c * P:(c + 1) * P], pt_p[:, NP_:384], start=False, stop=True)
            last.then_inc(sem("pv_ps"), 1)

        def q_of(r, b, c):
            return qs[0:RO, 2, 4 * r + b, :] if c == 2 else qs[:, c, 4 * r + b, :]

        def s_chunk(r, cc):
            u = cc % 2
            pe.wait_ge(sem(f"key_full{u}"), 128 * (2 * r + cc // 2 + 1))
            if cc == 0 and r == 1:
                pe.wait_ge(sem("s_pt_a"), 1)
                pe.wait_ge(sem("s_pt_d"), 2)
            if cc == 3 and r == 1:
                pe.wait_ge(sem("s_ol"), 2)
            if cc == 0 and r == 0:
                pe.wait_ge(sem("qs"), 3)
            for c in range(3):
                for b in range(4):
                    mov = keys[:, u, b, :, c * P:(c + 1) * P] if c < 2 else keys[0:RO, u, b, :, 256:384]
                    last = mm(ps[32 * b:32 * b + 32, 4 + cc // 2, (cc % 2) * 256:(cc % 2) * 256 + 256],
                              q_of(r, b, c), mov, start=(c == 0), stop=(c == 2))
            last.then_inc(sem("key_free"), 1)
            if cc == 3:
                for c in range(3):
                    for b in range(4):
                        mov = ckvT[:, c, NP_:T] if c < 2 else krT[:, NP_:T]
                        last = mm(ps[32 * b:32 * b + 32, 6, 0:NS_], q_of(r, b, c), mov, start=(c == 0), stop=(c == 2))
                last.then_inc(sem("s_ps"), 1)

        def s_turn(r):
            pe.wait_ge(sem("s_pn"), r + 1)
            for g in range(8):
                nc.tensor.transpose(ps[:, 4 + g // 4, (g % 4) * P:(g % 4) * P + P], p_s[:, g * P:(g + 1) * P], ident)
            nc.tensor.transpose(ps[0:NS_, 6, 0:P], p_s[:, PAST:PAST + NS_], ident).then_inc(sem("s_pt_ps"), 1)

        def v_chunk(r, cc):
            j = (4 * r + cc) % 7
            if cc == 0:
                pe.wait_ge(sem("s_pt_a"), r + 1)
                pe.wait_ge(sem("s_pt_d"), 2 * r + 2)
                pe.wait_ge(sem(f"rows_full{r}"), 32 * 16)
            for g in range(2):
                for b in range(4):
                    last = mm(ps[32 * b:32 * b + 32, 7, 0:KV], pt_s[:, 2 * cc + g, 32 * b:32 * b + 32],
                              ring(j, (2 * b + g) * KV, KV), start=(cc == 0 and g == 0), stop=False)
            last.then_inc(sem("rows_free"), 1)
            if cc == 3:
                for b in range(4):
                    last = mm(ps[32 * b:32 * b + 32, 7, 0:KV], pt_s[0:NS_, 8, 32 * b:32 * b + 32], ckt[0:NS_, 2, :], start=False, stop=True)
                last.then_inc(sem("s_o_ps"), 1)

        def s_out(r):
            pe.wait_ge(sem("s_ola"), r + 1)
            for c in range(2):
                last = nc.tensor.transpose(ps[:, 6, P + c * P:2 * P + c * P], ola_s[:, c * P:(c + 1) * P], ident)
            last.then_inc(sem("s_ot_ps"), 1)

        def head(h):
            turn_p(h)
            if h + 2 < H:
                if h == 5:
                    s_out(0)
                scores(h + 2)
            apply_p(h)

        scores(0), scores(1)
        s_chunk(0, 0), s_chunk(0, 1), head(0), head(1)
        s_chunk(0, 2), head(2)
        s_chunk(0, 3), head(3), s_turn(0)
        s_chunk(1, 0), v_chunk(0, 0), v_chunk(0, 1), head(4)
        s_chunk(1, 1), v_chunk(0, 2), v_chunk(0, 3), head(5)
        s_chunk(1, 2), head(6)
        s_chunk(1, 3), head(7)
        s_turn(1)
        for cc in range(4):
            v_chunk(1, cc)
        s_out(1)
        pe.wait_ge(sem("ol"), H)
        pe.wait_ge(sem("s_ol"), 4)
        wait_slots(pe, S_UV, S_UV + 1)
        for h in range(H):
            if h >= 4:
                pe.wait_ge(sem("o_a" if h % 2 == 0 else "o_d"), (h - 4) // 2 + 1)
            for c in range(2):
                last = mm(bank(h % 4, T), ring(S_UV, c * D + h * P, P), ql[:, h, c, :], start=(c == 0), stop=(c == 1))
            last.then_inc(sem("o_ps"), 1)
        owe(1)
        pe.wait_ge(sem("o_a"), H // 2)
        pe.wait_ge(sem("o_d"), H // 2)
        for m in range(KD):
            if m % 2 == 0:
                wait_slots(pe, S_O + m // 2, S_O + m // 2 + 1)
            if m >= 4:
                pe.wait_ge(sem("h_upd"), m - 3)
            for k in range(H):
                last = mm(bank(WO_BANK[m % 4], T), ring(S_O, m * D + k * P, P), oT[:, k, :], start=(k == 0), stop=(k == H - 1))
                if k == 0:
                    free_with(last)
            last.then_inc(sem("h_part"), 1)
            if m % 2 == 1:
                owe(1)
            if m >= 2:
                sum_sq("ffn0", hn_t, m - 2)

        def moe(L):
            norm(f"ffn{L}", hn_t, KD - 2)
            pe.wait_ge(sem("wr_in"), 32)
            for t, (t0, tn) in enumerate(TOK):
                for k in range(KD):
                    if t == 0:
                        pe.wait_ge(sem("hn"), N_BASE[f"ffn{L}"] + k + 1)
                    last = mm(ps[0:tn, 0, 36 * t:36 * t + 36], hn_t[:, k, t0:t0 + tn], w_r[:, L, k, :], start=(k == 0), stop=(k == KD - 1))
            last.then_inc(sem("lg_ps"), 1)
            for t, (t0, tn) in enumerate(TOK):
                if t == 2:
                    pe.wait_ge(sem("hr_a"), 3 * L + 1)
                for k in range(KD):
                    last = nc.tensor.transpose(ps[0:tn, 2 + 2 * (t % 2) + k // 4, (k % 4) * P:(k % 4) * P + P], hn_t[:, k, t0:t0 + tn], ident)
                last.then_inc(sem("hr_ps"), 1)
            pe.wait_ge(sem("sel"), L + 1)
            pe.wait_ge(sem("hr_a"), 3 * L + 3)
            lt = const[:, C_LT:C_LT + P]
            for t in range(3):
                for j in range(t):
                    mm(ps[:, 1, 32 * t:32 * t + 32], ones, sel[:, j, :], start=(j == 0), stop=False)
                last = mm(ps[:, 1, 32 * t:32 * t + 32], lt, sel[:, t, :], start=(t == 0), stop=True)
            last.then_inc(sem("rank_ps"), 1)
            for t, (t0, tn) in enumerate(TOK):
                last = mm(ps[:, 3, 0:32], ones[0:tn, :], sel[0:tn, t, :], start=(t == 0), stop=(t == 2))
            last.then_inc(sem("total_ps"), 1)
            pe.wait_ge(sem("pT_in"), 16 * L + 16)
            pe.wait_ge(sem("hr_a"), 3 * L + 3)
            wait_slots(pe, S_PROJ[L], S_PROJ[L] + 1)
            for m in range(KD):
                if m >= 4:
                    pe.wait_ge(sem("prj"), 8 * L + m - 3)
                for k in range(2):
                    last = mm(bank(4 + m % 4, T), ring(S_PROJ[L], m * 256 + k * P, P), pT[:, k, :], start=(k == 0), stop=(k == 1))
                last.then_inc(sem("prj_ps"), 1)
            pe.drain().then_inc(sem("slot_free"), 1)
            pe.wait_ge(sem("list_in"), 16 * L + 16)
            li = lst.rearrange("c (r v) -> c v r", v=2)
            for v in range(2):
                last = nc.tensor.transpose(ps[:, 2, P * v:P * v + COLS], li[:, v, :], ident[0:COLS, 0:COLS])
            last.then_inc(sem("lst_ps"), 1)
            pe.wait_ge(sem("slots"), L + 1)
            pe.wait_ge(sem("prj"), 8 * L + KD)

            def pair(i, b, tail):
                n1 = i * 2 + (b + 1)
                pe.wait_ge(sem(f"x_got{L}_{b}"), i * 16 + 16)
                for k in range(KD):
                    last = nc.tensor.transpose(ps[:, k // 4, (k % 4) * P:(k % 4) * P + P], x_sel[:, b, k * P:(k + 1) * P], ident)
                last.then_inc(sem(f"x_ps{L}"), 1)
                pe.wait_ge(sem(f"xT_a{L}"), n1)
                pe.wait_ge(sem(f"xT_d{L}"), n1)
                s0 = S_MOE[L] + 6 * b
                if tail is None:
                    for j in range(4):
                        pe.wait_ge(sem(f"slot_full{(s0 + j) % RING}"), i * 16 + 16 * ((s0 + j) // RING + 1))
                    gu = [ring(s0 + 2 * a, 0, 2 * SLOT) for a in range(2)]
                    dn = [ring(s0 + 4 + a, 0, SLOT) for a in range(2)]
                else:
                    pe.wait_ge(sem(f"tail_w{L}"), tail * 128 + 64 * (b + 1))
                    gu = [tail_gu[:, a].rearrange("p s n -> p (s n)") for a in range(2)]
                    dn = tail_dn
                for k in range(KD):
                    for a in range(2):
                        last = mm(ps[64 * a:64 * a + 64, 2 + b, :], xT[:, k, 64 * a:64 * a + 64], gu[a][:, k * 512:(k + 1) * 512],
                                  start=(k == 0), stop=(k == KD - 1))
                last.then_inc(sem(f"h_ps{L}"), 1)
                pe.wait_ge(sem(f"a{L}"), n1)
                for k in range(2):
                    last = nc.tensor.transpose(ps[:, 4, k * P:(k + 1) * P], act_a[:, k * P:(k + 1) * P], ident)
                    if k == 0 and tail is None:
                        last.then_inc(sem("slot_free"), 4)
                last.then_inc(sem(f"aT_ps{L}"), 1)
                pe.wait_ge(sem(f"aT{L}"), n1)
                pe.wait_ge(sem(f"y_a{L}"), n1)
                pe.wait_ge(sem(f"y_d{L}"), n1)
                if tail is None:
                    for j in (4, 5):
                        pe.wait_ge(sem(f"slot_full{(s0 + j) % RING}"), i * 16 + 16 * ((s0 + j) // RING + 1))
                for k in range(2):
                    for n in range(2):
                        for a in range(2):
                            last = mm(ps[64 * a:64 * a + 64, 5 + n, :], aT[:, k, 64 * a:64 * a + 64],
                                      dn[a][:, k * D + n * 512:k * D + n * 512 + 512], start=(k == 0), stop=(k == 1))
                last.then_inc(sem(f"y_ps{L}"), 1)
                if tail is None:
                    pe.drain().then_inc(sem("slot_free"), 2)

            with pe.Fori(0, PAIRS // 2) as i:
                for b in range(2):
                    pair(i, b, None)
            pe.wait_ge(sem("cnt"), L + 1)
            most = pe.value_load(cnt_i[0:1, L:L + 1], min_val=0, max_val=T)
            with pe.If(most > WIN):
                with pe.Fori(0, (PASSES - 1) * PAIRS // 2) as j:
                    for b in range(2):
                        pair(j + PAIRS // 2, b, j)
            pe.wait_ge(sem("comb"), 3 * L + 3)
            for k in range(KD):
                if k >= 4:
                    pe.wait_ge(sem("h_upd"), 8 * (1 if L == 0 else 4) + k - 3)
                for t, (t0, tn) in enumerate(TOK):
                    last = nc.tensor.transpose(ps[:, k % 4, t0:t0 + tn], y12[0:tn, 0, t, k * P:(k + 1) * P], ident[0:tn, 0:tn])
                last.then_inc(sem("h_part"), 1)
                if k >= 2:
                    sum_sq(f"ple{L}", hn_t, k - 2)
            norm(f"ple{L}", hn_t, KD - 2)
            for m in range(KD):
                s = S_GATE[L] + m // 2
                if m % 2 == 0:
                    wait_slots(pe, s, s + 1)
                if m >= 4:
                    pe.wait_ge(sem("pg_sig"), 8 * L + m - 3)
                for k in range(KD):
                    if m == 0:
                        pe.wait_ge(sem("hn"), N_BASE[f"ple{L}"] + k + 1)
                    last = mm(bank(m % 4, T), ring(s, (m % 2) * D + k * P, P), hn_t[:, k, :], start=(k == 0), stop=(k == KD - 1))
                    if k == 0:
                        free_with(last)
                last.then_inc(sem("pg_ps"), 1)
                if m == 2 and L == 0:
                    pe.wait_ge(sem("ws_m"), 2)
                    for g in range(8):
                        mm(ps[:, 5 + g // 4, (g % 4) * P:(g % 4) * P + P], ones, wsT[:, g, :], start=True, stop=True)
                    for g in range(8):
                        last = mm(ps[:, 4, 32 * g:32 * g + 32], ones[0:NS_, :], wsS[:, g, :], start=True, stop=True)
                    last.then_inc(sem("rs_ps"), 1)
                if m % 2 == 1:
                    owe(1)
                if m >= 2:
                    sum_sq(NEXT[L], prj, m - 2)
            norm(NEXT[L], prj, KD - 2)

        moe(0)

        def z_tile(i):
            s = S_SGU + i // 2
            if i % 2 == 0:
                wait_slots(pe, s, s + 1)
            if i >= 4:
                pe.wait_ge(sem("z_sb"), i - 3)
            for k in range(KD):
                if i == 0:
                    pe.wait_ge(sem("hn"), N_BASE["mix1"] + k + 1)
                last = mm(bank(i % 4, T), ring(s, (i % 2) * D + k * P, P), hn_t[:, k, :], start=(k == 0), stop=(k == KD - 1))
                if k == 0:
                    free_with(last)
            last.then_inc(sem("z_ps"), 1)
            if i % 2 == 1:
                owe(1)

        def v_turn(t):
            pe.wait_ge(sem("z_sb"), t + 1)
            if t < 2:
                pe.wait_ge(sem("rs"), 2)
            else:
                pe.wait_ge(sem("v_sb"), 2 * (t - 1))
            for j, (t0, tn) in enumerate(TOK):
                last = nc.tensor.transpose(ps[0:tn, 4 + t % 2, j * P:j * P + P], vT[:, t % 2, t0:t0 + tn], ident)
            last.then_inc(sem("vt_ps"), 1)

        def mix(t):
            if t == 0:
                pe.wait_ge(sem("v_n"), 3)
            if t >= 2:
                pe.wait_ge(sem("g_sb"), t - 1)
            fs = slice(t * P, (t + 1) * P)
            for j in range(2):
                mm(ps[:, 6 + t % 2, j * P:(j + 1) * P], v_tok[:, j, fs], wsT[:, t // 3, :], start=True, stop=True)
            mm(ps[:, 6 + t % 2, NP_:T], v_tok[0:NS_, 2, fs], wsS[:, t // 3, :], start=True, stop=True).then_inc(sem("sp_ps"), 1)

        for t in range(FT):
            z_tile(t)
            if t >= 1:
                v_turn(t - 1)
        LAG = 7
        for t in range(FT):
            z_tile(FT + t)
            if t == 0:
                v_turn(FT - 1)
            if t >= LAG:
                mix(t - LAG)
        for t in range(FT - LAG, FT):
            mix(t)
        pe.wait_ge(sem("v_sb"), 2 * FT)
        for t in range(FT):
            last = nc.tensor.transpose(ps[:, 4 + t // 16, (t % 16) * NS_:(t % 16) * NS_ + NS_], v_tok[0:NS_, 2, t * P:(t + 1) * P], ident[0:NS_, 0:NS_])
        last.then_inc(sem("vs_ps"), 1)
        pe.wait_ge(sem("z_sb"), 2 * FT)
        for m in range(KD):
            for k in range(FT):
                at = m * FT + k
                s = S_OUT + at // 16
                if at % 16 == 0:
                    wait_slots(pe, s, s + 1)
                if m == 0:
                    pe.wait_ge(sem("g_sb"), k + 1)
                if k == 0 and m >= 4:
                    pe.wait_ge(sem("h_upd"), 24 + m - 3)
                last = mm(bank(m % 4, T), ring(s, (at % 16) * P, P), uT[:, k, :], start=(k == 0), stop=(k == FT - 1))
                if k == 0:
                    free_with(last)
                if at % 16 == 15 and k != FT - 1:
                    last.then_inc(sem("slot_free"), 1)
            last.then_inc(sem("h_part"), 1)
            if (m * FT + FT) % 16 == 0:
                owe(1)
            if m >= 2:
                sum_sq("ffn1", hn_t, m - 2)
        moe(1)


def _tiles(w, cols):
    k = w.shape[0] // P
    return np.concatenate([w[:, c].reshape(k, P, -1).transpose(1, 0, 2).reshape(P, -1) for c in cols], 1)


def _slots(a):
    return a.reshape(P, -1, SLOT).transpose(1, 0, 2)


def _stream(i):
    cols = lambda n: [slice(c, c + P) for c in range(0, n, P)]
    swap = lambda c0: [*range(c0 + 32, c0 + 64), *range(c0, c0 + 32)]
    w_in, w_qb = i["mla_w_in"][0], i["mla_w_qb"][0]
    a = QL + KV
    parts = [_slots(_tiles(w_in, cols(a) + [slice(a, a + RO), swap(a)]))]
    q = [slice(192 * h, 192 * h + 128) for h in range(H)]
    for p in range(H // 2):
        r = [192 * (2 * p + j) + 128 for j in range(2)]
        q += [[*range(r[0], r[0] + RO), *range(r[1], r[1] + RO)], swap(r[0]) + swap(r[1])]
    parts.append(_slots(_tiles(w_qb, q)))
    parts.append(_slots(i["mla_w_uk"][0].transpose(2, 1, 0).reshape(P, -1)))
    parts.append(_slots(i["mla_w_uv"][0].reshape(2, P, -1).transpose(1, 0, 2).reshape(P, -1)))
    parts.append(_slots(_tiles(i["mla_w_o"][0], cols(D))))
    for L in range(2):
        parts.append(_slots(_tiles(i["ple_w_proj"][L], cols(D))))
        gu = np.concatenate([i["moe_w_gate"][L], i["moe_w_up"][L]], 2).reshape(NE, KD, P, 2 * FH)
        gu = gu.transpose(0, 2, 1, 3).reshape(PAIRS, 2, P, 2, SLOT).transpose(0, 1, 3, 2, 4).reshape(PAIRS, 4, P, SLOT)
        dn = i["moe_w_down"][L].reshape(PAIRS, 2, 2, P, D).transpose(0, 1, 3, 2, 4).reshape(PAIRS, 2, P, SLOT)
        parts.append(np.concatenate([gu, dn], 1).reshape(PAIRS * 6, P, SLOT))
        parts.append(_slots(_tiles(i["ple_w_gate"][L], cols(D))))
        if L == 0:
            w = i["sgu_w_in"][0]
            parts.append(_slots(_tiles(w, [slice(FF + c, FF + c + P) for c in range(0, FF, P)] + cols(FF))))
            parts.append(_slots(_tiles(i["sgu_w_out"][0], cols(D))))
    return np.concatenate(parts, 0)


def _constants():
    c, ac = np.zeros((P, N_CONST), np.float32), np.zeros((P, N_ACONST), np.float32)
    r, q = np.arange(P)[:, None], np.arange(P)[None, :]
    c[:, C_ID:C_ID + P] = np.eye(P)
    c[:, C_ONE:C_ONE + P] = 1
    for at in (0, 2 * P):
        ac[:, C_MSK + at:C_MSK + at + P] = np.where(q <= r, 0, NEG)
    rb, rs_, key = r // 32, r % DEC_S, np.arange(NS_)[None, :]
    for rnd in range(2):
        ok = (key // DEC_S == 4 * rnd + rb) & (key % DEC_S <= rs_)
        ac[:, C_SMSK + NS_ * rnd:C_SMSK + NS_ * (rnd + 1)] = np.where(ok, 0, NEG)
    c[:, C_LT:C_LT + P] = r < q
    c[:, C_WM:C_WM + P] = r <= q
    c[0:NS_, C_WSM:C_WSM + NS_] = ((r // DEC_S == q // DEC_S) & (r % DEC_S <= q % DEC_S))[0:NS_, 0:NS_]
    pos = np.concatenate([np.arange(NP_), np.tile(PAST + np.arange(DEC_S), DEC_B)]).astype(np.float32)
    inv = (1.0 / (np.float32(10000.0) ** (np.arange(0, RO, 2, dtype=np.float32) / np.float32(RO)))).astype(np.float32)
    ang = (pos[None, :] * inv[np.arange(P) % 32][:, None]).astype(np.float32)
    ac[:, C_COS:C_COS + T] = np.cos(ang)
    ac[:, C_SIN:C_SIN + T] = np.sin(ang) * np.where(np.arange(P) % 64 < 32, -1, 1)[:, None]
    c[:, C_IOTA:C_IOTA + EPG] = np.arange(EPG)
    c[NS_:, C_INV + 2] = 1e6
    for t in range(3):
        for k in range(2):
            c[:, C_TV + 4 * t + 2 * k] = P * t + np.arange(P)
            c[:, C_TV + 4 * t + 2 * k + 1] = k * T + P * t + np.arange(P)
    return c, ac


def _params(i):
    col = lambda v: v.reshape(-1, P).T
    return np.concatenate([col(v) for v in (
        i["g_mix"][0], i["g_mix"][1], i["g_ffn"][0], i["g_ffn"][1], i["g_ple"][0], i["g_ple"][1], i["g_final"],
        i["mla_g_q"][0], i["mla_g_kv"][0], i["sgu_b_in"][0], i["sgu_g_v"][0], i["sgu_b_v"][0])], 1)


def kernel(**inputs):
    import concourse.bacc as bacc
    from concourse.bass_utils import run_bass_kernel_spmd

    i = {k: np.asarray(v) for k, v in inputs.items()}
    feat = lambda a: a.T.reshape(-1, P, a.shape[0]).transpose(1, 0, 2)
    tok = lambda p, s: np.concatenate([p.reshape(NP_, -1), s.reshape(NS_, -1)], 0)
    ckv, kr = i["cache_ckv"][0], i["cache_krope"][0]
    n_phys = ckv.shape[0]
    key_pages = np.zeros((n_phys, P, 384), np.float32)
    key_pages[:, :, 0:256] = ckv.transpose(0, 2, 1).reshape(n_phys, 2, P, PAGE).transpose(0, 2, 1, 3).reshape(n_phys, P, 256)
    key_pages[:, 0:RO, 256:384] = kr.transpose(0, 2, 1)
    w_s, b_s = i["sgu_w_s"][0], i["sgu_b_s"][0]
    w_r = np.concatenate([i["moe_w_rg"], i["moe_w_re"]], 2)
    b_r = np.concatenate([i["moe_b_rg"], i["moe_b_re"]], 1)
    arrays = {
        "stream": _stream(i),
        "x": feat(tok(i["x_prompt"], i["x_sample"])),
        "p": np.stack([feat(tok(i["p_prompt"][L], i["p_sample"][L])) for L in range(2)], 1),
        "key_pages": key_pages,
        "row_pages": ckv,
        "ptab": i["page_table"].reshape(1, -1).astype(np.int32),
        "par": _params(i),
        "const": _constants()[0],
        "aconst": _constants()[1],
        "w_r": w_r.reshape(2, KD, P, G + NE).transpose(2, 0, 1, 3),
        "b_r": np.broadcast_to(b_r, (P, 2, G + NE)),
        "ws": w_s.transpose(2, 0, 1),
        "wss": np.tile(w_s[:, :DEC_S, :DEC_S].transpose(2, 0, 1), (DEC_B, 1, DEC_B)),
        "bs": np.broadcast_to(np.concatenate([b_s, np.tile(b_s[:, :DEC_S], (1, DEC_B))], 1), (P, 8, 160)),
    }
    arrays = {k: np.ascontiguousarray(v) for k, v in arrays.items()}
    nc = bacc.Bacc("TRN2", target_bir_lowering=False, num_devices=1)
    io = {k: nc.dram_tensor(k, v.shape, mybir.dt.from_np(v.dtype), kind="ExternalInput").ap() for k, v in arrays.items()}
    outs = {"y_out": (P, KD, T), "ckv_out": (P, 2, T), "kr_out": (RO, T), "vs_out": (P, FT, NS_)}
    for k, shape in outs.items():
        io[k] = nc.dram_tensor(k, shape, FP, kind="ExternalOutput").ap()
    io["lists"] = [nc.dram_tensor(f"list{L}", (COLS * P, 2), FP).ap() for L in range(2)]
    io["hn_rows"] = [nc.dram_tensor(f"hn_rows{L}", (T, D), FP).ap() for L in range(2)]
    io["y_rows"] = [nc.dram_tensor(f"y_rows{L}", (2 * T, D), FP).ap() for L in range(2)]
    io["n_phys"] = n_phys
    build(nc, io)
    got = run_bass_kernel_spmd(nc, [arrays], core_ids=[0]).results[0]
    rows = lambda a: a.transpose(2, 1, 0).reshape(a.shape[2], -1)
    y, c, v = rows(got["y_out"]), rows(got["ckv_out"]), rows(got["vs_out"])
    r = got["kr_out"].T
    new = (1, DEC_B, DEC_S, -1)
    return (y[:NP_].reshape(1, NP_, D), y[NP_:].reshape(DEC_B, DEC_S, D),
            c[:NP_].reshape(1, 1, NP_, KV), r[:NP_].reshape(1, 1, NP_, RO),
            c[NP_:].reshape(new), r[NP_:].reshape(new), v.reshape(new))
```
